# Optimizing a Trainium2 kernel written in Bass

```python
import jax, jax.numpy as jnp
from jax import lax
import numpy as np

D_MODEL = 1024
BATCH = 1
SEQ = 256
DEPTH = 2

PLE_DIM = 256
D_FF = 2816
EPS = 1e-6
ROPE_THETA = 10000.0
RET_THETA = 10000.0
N_NORMS = 7

A_HEADS = 4
A_DK = 128
A_DV = 128
A_CHUNK = 64
B_Q_HEADS = 8
B_KV_HEADS = 2
B_HEAD_DIM = 64
B_WINDOW = 128
B_BLOCK = 128
C_HEADS = 4
C_DK = 256
C_DV = 512
C_CHUNK = 128

N_EVEN = (DEPTH + 1) // 2
N_ODD = DEPTH // 2

A_KW = A_HEADS * A_DK
A_VW = A_HEADS * A_DV
B_QW = B_Q_HEADS * B_HEAD_DIM
B_KW = B_KV_HEADS * B_HEAD_DIM
EVEN_SPLITS = [A_KW, 2 * A_KW, 2 * A_KW + A_VW, 2 * A_KW + 2 * A_VW, 2 * A_KW + 2 * A_VW + B_QW,
               2 * A_KW + 2 * A_VW + B_QW + B_KW]
EVEN_IN = 2 * A_KW + 2 * A_VW + B_QW + 2 * B_KW
EVEN_OUT = A_VW + B_QW
C_KW = C_HEADS * C_DK
C_VW = C_HEADS * C_DV
ODD_SPLITS = [C_KW, 2 * C_KW, 2 * C_KW + C_VW]
ODD_IN = 2 * C_KW + 2 * C_VW
ODD_OUT = C_VW


def rmsnorm(x, g):
    xf = x.astype(jnp.float32)
    y = xf * lax.rsqrt(jnp.mean(xf * xf, axis=-1, keepdims=True) + EPS)
    return (y * g.astype(jnp.float32)).astype(x.dtype)

def swiglu(x, w_in, w_out):
    gate, up = jnp.split(x @ w_in, 2, axis=-1)
    return (jax.nn.silu(gate) * up) @ w_out

def rope_tables(positions, inv_freq):
    ang = positions.astype(jnp.float32)[:, :, None] * inv_freq[None, None, :]
    return jnp.cos(ang)[:, :, None, :], jnp.sin(ang)[:, :, None, :]

def apply_rope(x, cos, sin):
    xf = x.astype(jnp.float32)
    x1, x2 = jnp.split(xf, 2, axis=-1)
    return jnp.concatenate([x1 * cos - x2 * sin, x2 * cos + x1 * sin], axis=-1).astype(x.dtype)

def hgrn2_chunkwise(q, f_logit, i, lb):
    B, S, H, K = q.shape
    V = i.shape[-1]
    C = A_CHUNK
    n = S // C

    def chunks(t):
        return t.astype(jnp.float32).reshape(B, n, C, H, -1).transpose(0, 3, 1, 2, 4)

    lb5 = lb[None, :, None, None, :]
    qf = jax.nn.silu(chunks(q))
    f = lb5 + (1.0 - lb5) * jax.nn.sigmoid(chunks(f_logit))
    k = 1.0 - f
    v = chunks(i)
    b = jnp.cumsum(jnp.log(f), axis=3)
    b_last = b[:, :, :, -1:, :]
    q_s = qf * jnp.exp(b)
    k_s = k * jnp.exp(-b)
    k_d = k * jnp.exp(b_last - b)
    causal = jnp.tril(jnp.ones((C, C), dtype=bool))
    att = jnp.where(causal, jnp.einsum('bhnck,bhnsk->bhncs', q_s, k_s), 0.0)
    intra = jnp.einsum('bhncs,bhnsv->bhncv', att, v)
    dec = jnp.exp(b_last[:, :, :, 0, :])

    def step(state, xs):
        qc, kc, vc, dc = xs
        o = jnp.einsum('bhck,bhkv->bhcv', qc, state)
        state = state * dc[..., None] + jnp.einsum('bhck,bhcv->bhkv', kc, vc)
        return state, o

    xs = (jnp.moveaxis(q_s, 2, 0), jnp.moveaxis(k_d, 2, 0), jnp.moveaxis(v, 2, 0), jnp.moveaxis(dec, 2, 0))
    _, inter = lax.scan(step, jnp.zeros((B, H, K, V), jnp.float32), xs)
    o = intra + jnp.moveaxis(inter, 0, 2)
    return o.transpose(0, 2, 3, 1, 4).reshape(B, S, H, V)

def swa_with_sinks(q, k, v, sinks):
    B, S, Hq, D = q.shape
    G = k.shape[2]
    R = Hq // G
    L = B_BLOCK
    nb = S // L
    qb = q.reshape(B, nb, L, G, R, D)
    kb = k.reshape(B, nb, L, G, D)
    vb = v.reshape(B, nb, L, G, D)
    pad = ((0, 0), (1, 0), (0, 0), (0, 0), (0, 0))
    kk = jnp.concatenate([jnp.pad(kb[:, :-1], pad), kb], axis=2)
    vv = jnp.concatenate([jnp.pad(vb[:, :-1], pad), vb], axis=2)
    s = jnp.einsum('bnqgrd,bnkgd->bngrqk', qb, kk).astype(jnp.float32) * (D ** -0.5)
    qi = jnp.arange(L)[:, None]
    kj = jnp.arange(2 * L)[None, :]
    diff = qi + L - kj
    band = (diff >= 0) & (diff < B_WINDOW)
    key_pos = jnp.arange(nb)[:, None, None] * L - L + kj[None]
    valid = band[None] & (key_pos >= 0)
    s = jnp.where(valid[None, :, None, None], s, -jnp.inf)
    sink = sinks.astype(jnp.float32).reshape(G, R)[None, None, :, :, None, None]
    m = jnp.maximum(jnp.max(s, axis=-1, keepdims=True), sink)
    pr = jnp.exp(s - m)
    denom = jnp.sum(pr, axis=-1, keepdims=True) + jnp.exp(sink - m)
    o = jnp.einsum('bngrqk,bnkgd->bnqgrd', (pr / denom).astype(vv.dtype), vv)
    return o.reshape(B, S, Hq * D)

def retention_chunkwise(q, k, v):
    B, S, H, K = q.shape
    V = v.shape[-1]
    C = C_CHUNK
    n = S // C
    lg = jnp.log1p(-jnp.exp2(-5.0 - jnp.arange(H, dtype=jnp.float32)))

    def chunks(t):
        return t.astype(jnp.float32).reshape(B, n, C, H, -1).transpose(0, 3, 1, 2, 4)

    qc = chunks(q)
    kc = chunks(k) * (K ** -0.5)
    vc = chunks(v)
    idx = jnp.arange(C, dtype=jnp.float32)
    diff = idx[:, None] - idx[None, :]
    decay = jnp.where(diff >= 0, jnp.exp(jnp.maximum(diff, 0.0)[None] * lg[:, None, None]), 0.0)
    att = jnp.einsum('bhnck,bhnsk->bhncs', qc, kc) * decay[None, :, None]
    intra = jnp.einsum('bhncs,bhnsv->bhncv', att, vc)
    q_in = qc * jnp.exp((idx + 1.0)[None, :] * lg[:, None])[None, :, None, :, None]
    k_in = kc * jnp.exp((C - 1.0 - idx)[None, :] * lg[:, None])[None, :, None, :, None]
    chunk_dec = jnp.exp(C * lg)[None, :, None, None]

    def step(state, xs):
        qx, kx, vx = xs
        o = jnp.einsum('bhck,bhkv->bhcv', qx, state)
        state = state * chunk_dec + jnp.einsum('bhck,bhcv->bhkv', kx, vx)
        return state, o

    xs = (jnp.moveaxis(q_in, 2, 0), jnp.moveaxis(k_in, 2, 0), jnp.moveaxis(vc, 2, 0))
    _, inter = lax.scan(step, jnp.zeros((B, H, K, V), jnp.float32), xs)
    o = intra + jnp.moveaxis(inter, 0, 2)
    return o.transpose(0, 2, 3, 1, 4).reshape(B, S, H, V)

def even_mixer(u, w_in, w_out, lb, onorm_g, sinks, cos_b, sin_b):
    B, S, _ = u.shape
    qa, fa, ia, ga, qb, kb, vb = jnp.split(u @ w_in, EVEN_SPLITS, axis=-1)
    oa = hgrn2_chunkwise(qa.reshape(B, S, A_HEADS, A_DK), fa.reshape(B, S, A_HEADS, A_DK),
                         ia.reshape(B, S, A_HEADS, A_DV), lb.reshape(A_HEADS, A_DK))
    oa = rmsnorm(oa, onorm_g) * jax.nn.silu(ga.reshape(B, S, A_HEADS, A_DV).astype(jnp.float32))
    oa = oa.reshape(B, S, A_VW).astype(u.dtype)
    qh = apply_rope(qb.reshape(B, S, B_Q_HEADS, B_HEAD_DIM), cos_b, sin_b)
    kh = apply_rope(kb.reshape(B, S, B_KV_HEADS, B_HEAD_DIM), cos_b, sin_b)
    ob = swa_with_sinks(qh, kh, vb.reshape(B, S, B_KV_HEADS, B_HEAD_DIM), sinks).astype(u.dtype)
    return jnp.concatenate([oa, ob], axis=-1) @ w_out

def odd_mixer(u, w_in, w_out, onorm_g, cos_c, sin_c):
    B, S, _ = u.shape
    qc, kc, vc, gc = jnp.split(u @ w_in, ODD_SPLITS, axis=-1)
    qh = apply_rope(qc.reshape(B, S, C_HEADS, C_DK), cos_c, sin_c)
    kh = apply_rope(kc.reshape(B, S, C_HEADS, C_DK), cos_c, sin_c)
    o = retention_chunkwise(qh, kh, vc.reshape(B, S, C_HEADS, C_DV))
    o = rmsnorm(o, onorm_g) * jax.nn.silu(gc.reshape(B, S, C_HEADS, C_DV).astype(jnp.float32))
    return o.reshape(B, S, C_VW).astype(u.dtype) @ w_out

def first_inputs(seed: int = 0) -> dict:
    key = jax.random.key(seed)
    ks = jax.random.split(key, 18)
    f32 = jnp.float32

    def w(k, shape, fan_in):
        return jax.random.normal(k, shape, f32) * (fan_in ** -0.5)

    x = jax.random.normal(ks[0], (BATCH, SEQ, D_MODEL), f32)
    p = jax.random.normal(ks[1], (DEPTH, BATCH, SEQ, PLE_DIM), f32)
    offsets = jax.random.randint(ks[2], (BATCH, 1), 0, 4096, dtype=jnp.int32)
    positions = (offsets + jnp.arange(SEQ, dtype=jnp.int32)[None, :]).astype(jnp.int32)
    norm_g = 1.0 + 0.05 * jax.random.normal(ks[3], (DEPTH, N_NORMS, D_MODEL), f32)
    ffn1_w_in = w(ks[4], (DEPTH, D_MODEL, 2 * D_FF), D_MODEL)
    ffn1_w_out = w(ks[5], (DEPTH, D_FF, D_MODEL), D_FF)
    ffn2_w_in = w(ks[6], (DEPTH, D_MODEL, 2 * D_FF), D_MODEL)
    ffn2_w_out = w(ks[7], (DEPTH, D_FF, D_MODEL), D_FF)
    ple_w_proj = w(ks[8], (DEPTH, PLE_DIM, D_MODEL), PLE_DIM)
    ple_w_gate = w(ks[9], (DEPTH, D_MODEL, D_MODEL), D_MODEL)
    even_w_in = w(ks[10], (N_EVEN, D_MODEL, EVEN_IN), D_MODEL)
    even_w_out = w(ks[11], (N_EVEN, EVEN_OUT, D_MODEL), EVEN_OUT)
    hgrn_lb = 0.1 * jax.random.normal(ks[12], (N_EVEN + 1, A_KW), f32)
    hgrn_onorm_g = 1.0 + 0.05 * jax.random.normal(ks[13], (N_EVEN, A_DV), f32)
    attn_sinks = jax.random.normal(ks[14], (N_EVEN, B_Q_HEADS), f32)
    odd_w_in = w(ks[15], (N_ODD, D_MODEL, ODD_IN), D_MODEL)
    odd_w_out = w(ks[16], (N_ODD, ODD_OUT, D_MODEL), ODD_OUT)
    ret_onorm_g = 1.0 + 0.05 * jax.random.normal(ks[17], (N_ODD, C_DV), f32)
    return {'x': x, 'p': p, 'positions': positions, 'norm_g': norm_g,
            'ffn1_w_in': ffn1_w_in, 'ffn1_w_out': ffn1_w_out, 'ffn2_w_in': ffn2_w_in, 'ffn2_w_out': ffn2_w_out,
            'ple_w_proj': ple_w_proj, 'ple_w_gate': ple_w_gate,
            'even_w_in': even_w_in, 'even_w_out': even_w_out, 'hgrn_lb': hgrn_lb, 'hgrn_onorm_g': hgrn_onorm_g,
            'attn_sinks': attn_sinks, 'odd_w_in': odd_w_in, 'odd_w_out': odd_w_out, 'ret_onorm_g': ret_onorm_g}

def first_block(x, p, positions, norm_g, ffn1_w_in, ffn1_w_out, ffn2_w_in, ffn2_w_out, ple_w_proj, ple_w_gate,
              even_w_in, even_w_out, hgrn_lb, hgrn_onorm_g, attn_sinks, odd_w_in, odd_w_out, ret_onorm_g):
    inv_b = ROPE_THETA ** (-jnp.arange(0, B_HEAD_DIM, 2, dtype=jnp.float32) / B_HEAD_DIM)
    inv_c = RET_THETA ** (-jnp.linspace(0.0, 1.0, C_DK // 2, dtype=jnp.float32))
    cos_b, sin_b = rope_tables(positions, inv_b)
    cos_c, sin_c = rope_tables(positions, inv_c)
    lb_all = jnp.cumsum(jax.nn.softmax(hgrn_lb.astype(jnp.float32), axis=0), axis=0)
    h = x
    for i in range(DEPTH):
        g = norm_g[i]
        h = h + 0.5 * rmsnorm(swiglu(rmsnorm(h, g[0]), ffn1_w_in[i], ffn1_w_out[i]), g[1])
        u = rmsnorm(h, g[2])
        j = i // 2
        if i % 2 == 0:
            mix = even_mixer(u, even_w_in[j], even_w_out[j], lb_all[j], hgrn_onorm_g[j], attn_sinks[j], cos_b, sin_b)
        else:
            mix = odd_mixer(u, odd_w_in[j], odd_w_out[j], ret_onorm_g[j], cos_c, sin_c)
        h = h + rmsnorm(mix, g[3])
        h = h + 0.5 * rmsnorm(swiglu(rmsnorm(h, g[4]), ffn2_w_in[i], ffn2_w_out[i]), g[5])
        gate = jax.nn.sigmoid(h @ ple_w_gate[i])
        h = h + rmsnorm(gate * (p[i] @ ple_w_proj[i]), g[6])
    return h


GRID_W = 64
CTX_LEN = 256
N_MIXERS = 3
POOL_WINDOWS = (2, 4, 8, 16)
POOL_GROUPS = 4
POOL_GW = D_MODEL // POOL_GROUPS
HEAD_DIM = 128
N_HEADS = D_MODEL // HEAD_DIM
N_KV_HEADS = N_HEADS // 2
QKV_WIDTH = (N_HEADS + 2 * N_KV_HEADS) * HEAD_DIM
ROPE_BASE = 10000.0
Q_BLOCK = 128
CHUNK = 128
GMLP_HALF = 2 * D_MODEL
GMLP_GROUPS = 8
GMLP_GW = GMLP_HALF // GMLP_GROUPS
D_FF_2 = 4 * D_MODEL


def n_layers_of(kind):
    return len(range(kind, DEPTH, N_MIXERS))

def rms_norm(x, g):
    xf = x.astype(jnp.float32)
    y = xf * lax.rsqrt(jnp.mean(xf * xf, axis=-1, keepdims=True) + EPS)
    return (y * g.astype(jnp.float32)).astype(x.dtype)

def layer_norm(x, g, b):
    xf = x.astype(jnp.float32)
    mu = jnp.mean(xf, axis=-1, keepdims=True)
    xc = xf - mu
    y = xc * lax.rsqrt(jnp.mean(xc * xc, axis=-1, keepdims=True) + EPS)
    return (y * g.astype(jnp.float32) + b.astype(jnp.float32)).astype(x.dtype)

def modulate(h, shift, scale):
    return h * (1 + scale[:, None, :]) + shift[:, None, :]

def pool_mix(h, w, scale):
    B, L, D = h.shape
    hf = h.astype(jnp.float32)
    cs = jnp.concatenate([jnp.zeros((B, 1, D), jnp.float32), jnp.cumsum(hf, axis=1)], axis=1)
    csg = cs.reshape(B, L + 1, POOL_GROUPS, POOL_GW)
    hg = hf.reshape(B, L, POOL_GROUPS, POOL_GW)
    pos = jnp.arange(L)
    outs = []
    for g, win in enumerate(POOL_WINDOWS):
        lo = jnp.clip(pos - win // 2, 0, L)
        hi = jnp.clip(pos + win - win // 2, 0, L)
        s = jnp.take(csg[:, :, g], hi, axis=1) - jnp.take(csg[:, :, g], lo, axis=1)
        cnt = (hi - lo).astype(jnp.float32)[None, :, None]
        outs.append(s / cnt - hg[:, :, g])
    p = jnp.stack(outs, axis=2).astype(h.dtype)
    y = jnp.einsum("blgc,gcd->blgd", p, w).reshape(B, L, D)
    return y * scale

def axial_rope_tables(L):
    rows_n = L // GRID_W
    row = jnp.repeat(jnp.arange(rows_n), GRID_W).astype(jnp.float32)
    col = jnp.tile(jnp.arange(GRID_W), rows_n).astype(jnp.float32)
    half = HEAD_DIM // 2
    inv = ROPE_BASE ** (-jnp.arange(0, half, 2, dtype=jnp.float32) / half)
    ang_r = row[:, None] * inv[None, :]
    ang_c = col[:, None] * inv[None, :]
    return jnp.cos(ang_r), jnp.sin(ang_r), jnp.cos(ang_c), jnp.sin(ang_c)

def rotate(x, cos, sin):
    x1, x2 = jnp.split(x, 2, axis=-1)
    cos = cos[None, :, None, :]
    sin = sin[None, :, None, :]
    return jnp.concatenate([x1 * cos - x2 * sin, x1 * sin + x2 * cos], axis=-1)

def apply_axial_rope(x, tables):
    cr, sr, cc, scol = tables
    xf = x.astype(jnp.float32)
    xr, xc = jnp.split(xf, 2, axis=-1)
    return jnp.concatenate([rotate(xr, cr, sr), rotate(xc, cc, scol)], axis=-1).astype(x.dtype)

def gqa_core(q, k, v):
    B, Lq = q.shape[0], q.shape[1]
    G = N_HEADS // N_KV_HEADS
    qg = q.reshape(B, Lq, N_KV_HEADS, G, HEAD_DIM)
    s = jnp.einsum("bqkgd,bskd->bkgqs", qg, k).astype(jnp.float32) * (HEAD_DIM ** -0.5)
    p = jax.nn.softmax(s, axis=-1).astype(v.dtype)
    o = jnp.einsum("bkgqs,bskd->bqkgd", p, v)
    return o.reshape(B, Lq, N_HEADS * HEAD_DIM)

def qkv_proj(h, w_qkv, q_g, k_g):
    B, L, _ = h.shape
    qkv = h @ w_qkv
    q, k, v = jnp.split(qkv, [N_HEADS * HEAD_DIM, (N_HEADS + N_KV_HEADS) * HEAD_DIM], axis=-1)
    q = rms_norm(q.reshape(B, L, N_HEADS, HEAD_DIM), q_g)
    k = rms_norm(k.reshape(B, L, N_KV_HEADS, HEAD_DIM), k_g)
    v = v.reshape(B, L, N_KV_HEADS, HEAD_DIM)
    return q, k, v

def attn_mix(h_ctx, h_lat, w_qkv, w_o, q_g, k_g, ctx_out):
    B, S, _ = h_lat.shape
    qc, kc, vc = qkv_proj(h_ctx, w_qkv, q_g, k_g)
    ql, kl, vl = qkv_proj(h_lat, w_qkv, q_g, k_g)
    tables = axial_rope_tables(S)
    ql = apply_axial_rope(ql, tables)
    kl = apply_axial_rope(kl, tables)
    k_all = jnp.concatenate([kc, kl], axis=1)
    v_all = jnp.concatenate([vc, vl], axis=1)
    nb = S // Q_BLOCK
    qb = ql.reshape(B, nb, Q_BLOCK, N_HEADS, HEAD_DIM).transpose(1, 0, 2, 3, 4)
    ob = lax.map(lambda qq: gqa_core(qq, k_all, v_all), qb)
    y_lat = ob.transpose(1, 0, 2, 3).reshape(B, S, N_HEADS * HEAD_DIM) @ w_o
    y_ctx = gqa_core(qc, kc, vc) @ w_o if ctx_out else None
    return y_ctx, y_lat

def gmlp_mix(h, w_in, ln_g, ln_b, ws, bs, w_out):
    B, L, _ = h.shape
    z = jax.nn.gelu(h @ w_in)
    u, v = jnp.split(z, 2, axis=-1)
    v = layer_norm(v, ln_g, ln_b)
    vg = v.reshape(B, L // CHUNK, CHUNK, GMLP_GROUPS, GMLP_GW)
    sv = jnp.einsum("gqp,bnpgc->bnqgc", ws, vg) + bs.T[None, None, :, :, None]
    return (u * sv.reshape(B, L, GMLP_HALF)) @ w_out

def sq_relu_mlp(h, w1, w2):
    return jnp.square(jax.nn.relu(h @ w1)) @ w2

def second_inputs(seed: int = 0) -> dict:
    key = jax.random.key(seed)
    ks = jax.random.split(key, 24)
    f32 = jnp.float32
    D = D_MODEL
    nP, nA, nG = n_layers_of(0), n_layers_of(1), n_layers_of(2)

    def nrm(k, shape, s):
        return jax.random.normal(k, shape, f32) * s

    return {
        "x": nrm(ks[0], (BATCH, SEQ, D), 1.0),
        "c": nrm(ks[1], (BATCH, D), 1.0),
        "ctx": nrm(ks[2], (BATCH, CTX_LEN, D), 1.0),
        "c_ctx": nrm(ks[3], (D,), 1.0),
        "ada_w": nrm(ks[4], (DEPTH, D, 6 * D), 0.5 * D ** -0.5),
        "ada_b": nrm(ks[5], (DEPTH, 6 * D), 0.02),
        "norm_g": 1.0 + nrm(ks[6], (DEPTH, 2, D), 0.02),
        "mlp_w1": nrm(ks[7], (DEPTH, D, D_FF_2), D ** -0.5),
        "mlp_w2": nrm(ks[8], (DEPTH, D_FF_2, D), D_FF_2 ** -0.5),
        "pool_w": nrm(ks[9], (nP, POOL_GROUPS, POOL_GW, POOL_GW), POOL_GW ** -0.5),
        "pool_scale": 1.0 + nrm(ks[10], (nP, D), 0.02),
        "attn_w_qkv": nrm(ks[11], (nA, D, QKV_WIDTH), D ** -0.5),
        "attn_w_o": nrm(ks[12], (nA, N_HEADS * HEAD_DIM, D), (N_HEADS * HEAD_DIM) ** -0.5),
        "attn_q_g": 1.0 + nrm(ks[13], (nA, HEAD_DIM), 0.02),
        "attn_k_g": 1.0 + nrm(ks[14], (nA, HEAD_DIM), 0.02),
        "gm_w_in": nrm(ks[15], (nG, D, 2 * GMLP_HALF), D ** -0.5),
        "gm_ln_g": 1.0 + nrm(ks[16], (nG, GMLP_HALF), 0.02),
        "gm_ln_b": nrm(ks[17], (nG, GMLP_HALF), 0.02),
        "gm_ws": nrm(ks[18], (nG, GMLP_GROUPS, CHUNK, CHUNK), CHUNK ** -0.5),
        "gm_bs": nrm(ks[19], (nG, GMLP_GROUPS, CHUNK), 0.02),
        "gm_w_out": nrm(ks[20], (nG, GMLP_HALF, D), GMLP_HALF ** -0.5),
        "final_g": 1.0 + nrm(ks[21], (D,), 0.02),
    }

def second_block(x, c, ctx, c_ctx, ada_w, ada_b, norm_g, mlp_w1, mlp_w2, pool_w, pool_scale,
              attn_w_qkv, attn_w_o, attn_q_g, attn_k_g, gm_w_in, gm_ln_g, gm_ln_b, gm_ws, gm_bs,
              gm_w_out, final_g):
    last_ctx_read = max([i for i in range(DEPTH) if i % N_MIXERS == 1], default=-1)
    s_lat = jax.nn.silu(c)
    s_ctx = jax.nn.silu(c_ctx)[None, :]
    h_lat, h_ctx = x, ctx
    for i in range(DEPTH):
        kind, j = i % N_MIXERS, i // N_MIXERS
        ctx_in = i <= last_ctx_read
        ctx_out = i < last_ctx_read
        sh1, sc1, g1, sh2, sc2, g2 = jnp.split(s_lat @ ada_w[i] + ada_b[i], 6, axis=-1)
        a_l = modulate(rms_norm(h_lat, norm_g[i, 0]), sh1, sc1)
        if ctx_in:
            csh1, csc1, cg1, csh2, csc2, cg2 = jnp.split(s_ctx @ ada_w[i] + ada_b[i], 6, axis=-1)
            a_c = modulate(rms_norm(h_ctx, norm_g[i, 0]), csh1, csc1)
        y_c = None
        if kind == 0:
            y_l = pool_mix(a_l, pool_w[j], pool_scale[j])
            if ctx_out:
                y_c = pool_mix(a_c, pool_w[j], pool_scale[j])
        elif kind == 1:
            y_c, y_l = attn_mix(a_c, a_l, attn_w_qkv[j], attn_w_o[j], attn_q_g[j], attn_k_g[j], ctx_out)
        else:
            y_l = gmlp_mix(a_l, gm_w_in[j], gm_ln_g[j], gm_ln_b[j], gm_ws[j], gm_bs[j], gm_w_out[j])
            if ctx_out:
                y_c = gmlp_mix(a_c, gm_w_in[j], gm_ln_g[j], gm_ln_b[j], gm_ws[j], gm_bs[j], gm_w_out[j])
        h_lat = h_lat + g1[:, None, :] * y_l
        m_l = modulate(rms_norm(h_lat, norm_g[i, 1]), sh2, sc2)
        h_lat = h_lat + g2[:, None, :] * sq_relu_mlp(m_l, mlp_w1[i], mlp_w2[i])
        if ctx_out:
            h_ctx = h_ctx + cg1[:, None, :] * y_c
            m_c = modulate(rms_norm(h_ctx, norm_g[i, 1]), csh2, csc2)
            h_ctx = h_ctx + cg2[:, None, :] * sq_relu_mlp(m_c, mlp_w1[i], mlp_w2[i])
    return rms_norm(h_lat, final_g)


def setup_inputs(seed=0):
    out = dict(first_inputs(seed))
    for name, value in second_inputs(seed + 1).items():
        if name != "x":
            out[name + "_2"] = value
    return out


def reference(
    x, p, positions, norm_g, ffn1_w_in, ffn1_w_out, ffn2_w_in, ffn2_w_out, ple_w_proj,
    ple_w_gate, even_w_in, even_w_out, hgrn_lb, hgrn_onorm_g, attn_sinks, odd_w_in, odd_w_out,
    ret_onorm_g, c_2, ctx_2, c_ctx_2, ada_w_2, ada_b_2, norm_g_2, mlp_w1_2, mlp_w2_2, pool_w_2,
    pool_scale_2, attn_w_qkv_2, attn_w_o_2, attn_q_g_2, attn_k_g_2, gm_w_in_2, gm_ln_g_2,
    gm_ln_b_2, gm_ws_2, gm_bs_2, gm_w_out_2, final_g_2,
):
    x = first_block(
        x, p, positions, norm_g, ffn1_w_in, ffn1_w_out, ffn2_w_in, ffn2_w_out, ple_w_proj,
        ple_w_gate, even_w_in, even_w_out, hgrn_lb, hgrn_onorm_g, attn_sinks, odd_w_in,
        odd_w_out, ret_onorm_g,
    )
    return second_block(
        x, c_2, ctx_2, c_ctx_2, ada_w_2, ada_b_2, norm_g_2, mlp_w1_2, mlp_w2_2, pool_w_2,
        pool_scale_2, attn_w_qkv_2, attn_w_o_2, attn_q_g_2, attn_k_g_2, gm_w_in_2, gm_ln_g_2,
        gm_ln_b_2, gm_ws_2, gm_bs_2, gm_w_out_2, final_g_2,
    )


_drawn_inputs = setup_inputs


def setup_inputs(seed=0):
    import zlib

    import numpy as np

    out = dict(_drawn_inputs(seed))
    spreads = {}
    factors = {'hgrn_lb': 5.278,
     'ctx_2': 8.0,
     'ada_b_2': 2.848,
     'norm_g_2': 8.0,
     'pool_scale_2': 8.0,
     'attn_q_g_2': 8.0,
     'attn_k_g_2': 8.0,
     'final_g_2': 2.838}
    for name, (base, spread) in spreads.items():
        noise = np.random.default_rng([zlib.crc32(name.encode()), seed]).standard_normal(out[name].shape)
        drawn = base * np.exp(spread * noise) if base else spread * noise
        out[name] = __import__('jax').numpy.asarray(drawn.astype(out[name].dtype))
    for name, factor in factors.items():
        out[name] = (out[name] * factor).astype(out[name].dtype)
    return out
```

```python
from contextlib import ExitStack

import numpy as np

import concourse.bass as bass
from concourse import mybir

F32 = mybir.dt.float32
F32R = mybir.dt.float32r
I32 = mybir.dt.int32
ACT = mybir.ActivationFunctionType
ALU = mybir.AluOpType
AX_X = mybir.AxisListType.X

P = 128
D = 1024
KT = D // P
SEQ = 256
MT = SEQ // P
SLAB = 2048
NSLOT = 3
EPS = 1e-6
D_FF = 2816
FFN_STEPS = D_FF // 256
MLP_H = 4096
MLP_STEPS = MLP_H // 512
EVEN_IN = 2816
ODD_IN = 6144
ADA_W = 6 * D
ADA_T = ADA_W // P
N_NORMS = 7

C_IDENT, C_TRI, C_SUF, C_IND, C_SWA, C_INV, C_SEL, C_AX, C_END = np.cumsum(
    [0, 128, 128, 128, 2, 256, 160, 2, 256]).tolist()


def shape_tables():
    p = np.arange(P)
    t = np.zeros((P, C_END), np.float32)
    t[:, C_IDENT:C_TRI] = np.eye(P)
    same = (p[:, None] // 64) == (p[None, :] // 64)
    t[:, C_TRI:C_SUF] = same & (p[:, None] <= p[None, :])
    t[:, C_SUF:C_IND] = same & (p[:, None] > p[None, :])
    t[:, C_IND:C_SWA] = (p[:, None] // 64) == np.arange(2)[None, :]
    big = np.float32(-1e30)
    t[:, C_SWA:C_SWA + 128] = np.where(p[None, :] > p[:, None], 0, big)
    t[:, C_SWA + 128:C_INV] = np.where(p[None, :] <= p[:, None], 0, big)
    inv_b = np.float32(10000.0) ** (-np.arange(0, 64, 2, dtype=np.float32) / np.float32(64))
    inv_c = np.float32(10000.0) ** (-np.linspace(0.0, 1.0, 128, dtype=np.float32))
    t[:, C_INV:C_SEL] = np.concatenate([inv_b, inv_c])[None]
    t[0:4, C_SEL:C_AX] = np.array([[1, 0], [0, 1], [1, 0], [0, 1]])
    tok = np.arange(SEQ)
    inv = np.float32(10000.0) ** (-np.arange(0, 64, 2, dtype=np.float32) / np.float32(64))
    row = (tok // 64).astype(np.float32)[:, None] * inv
    col = (tok % 64).astype(np.float32)[:, None] * inv
    ax = np.stack([np.cos(row), np.cos(col), np.sin(row), np.sin(col)], 1).reshape(MT, P, 128)
    t[:, C_AX:C_END] = ax.transpose(1, 0, 2).reshape(P, 256)

    lg = np.log1p(-np.exp2(-5.0 - np.arange(4)))
    diff = (p[None, :] - p[:, None]).astype(np.float64)
    same_c = np.where(diff[None] >= 0, np.exp(np.maximum(diff, 0)[None] * lg[:, None, None]), 0)
    cross = np.exp((diff + 128)[None] * lg[:, None, None])
    decay = np.stack([same_c, cross], 1) * 256 ** -0.5
    decay = np.ascontiguousarray(decay.transpose(2, 0, 1, 3).reshape(P, 1024).astype(np.float32))

    cnt = []
    for win in (2, 4, 8, 16):
        lo = np.clip(tok - win // 2, 0, SEQ)
        hi = np.clip(tok + win - win // 2, 0, SEQ)
        cnt.append(1.0 / (hi - lo))
    pool = np.broadcast_to(np.stack(cnt).reshape(1, 1024), (P, 1024)).astype(np.float32)
    return t, decay, np.ascontiguousarray(pool)


class Ring:

    def __init__(self):
        self.next, self.more = 0, 0

    def back(self, k):
        g = self.next - k
        return g % NSLOT, g // NSLOT + 1 + self.more

    def take(self):
        self.next += 1
        return self.back(1)

    def pairs(self, eng, n, body):
        with eng.Fori(0, n // 6) as t:
            self.more = 4 * t
            for u in range(6):
                body(6 * t + u, 4 + 2 * (u % 2))
        self.more = 0
        self.next += (n // 6 - 1) * 12

    def loop(self, eng, n, per, body):
        with eng.Fori(0, n // NSLOT) as t:
            self.more = per * t
            for u in range(NSLOT):
                body(NSLOT * t + u)
        self.more = 0
        self.next += (n // NSLOT - 1) * NSLOT * per
        for i in range(n - n % NSLOT, n):
            body(i)


def build(nc, T, out):
    with ExitStack() as ctx:
        def sb(name, shape, dt=F32):
            return ctx.enter_context(nc.sbuf_tensor(name, shape, dt))

        sems = {}

        def S(name):
            if name not in sems:
                sems[name] = ctx.enter_context(nc.semaphore(name))
            return sems[name]

        raw = sb("raw", [P, NSLOT, SLAB])
        w_hi = sb("w_hi", [P, NSLOT, SLAB], F32R)
        w_lo = sb("w_lo", [P, NSLOT, SLAB], F32R)
        h_lat = sb("h_lat", [P, MT, D])
        h_ctx = sb("h_ctx", [P, MT, D])
        xt_hi = sb("xt_hi", [P, KT, SEQ], F32R)
        xt_lo = sb("xt_lo", [P, KT, SEQ], F32R)
        ht_hi = sb("ht_hi", [P, 4, SEQ], F32R)
        ht_lo = sb("ht_lo", [P, 4, SEQ], F32R)
        s4 = sb("s4", [P, KT, P], F32R)
        arena = sb("arena", [P, 15360])
        tmp = sb("tmp", [P, 2048])
        gain = sb("gain", [P, D])
        table = sb("table", [P, 1024])
        const = sb("const", [P, C_END])
        norm_t = sb("norm_t", [P, 2 * N_NORMS * KT])
        adab_t = sb("adab_t", [P, 2 * ADA_T])
        vec_t = sb("vec_t", [P, 56])
        ada_t = sb("ada_t", [P, 2 * ADA_T, 2])
        mod = sb("mod", [P, 2, 2, 2, KT])
        rope_cos = sb("rope_cos", [P, MT, 160])
        rope_sin = sb("rope_sin", [P, MT, 160])
        ssq = sb("ssq", [P, 4, MT])
        rstd = sb("rstd", [P, 4, MT])
        ssq_h = sb("ssq_h", [P, 32])
        rstd_h = sb("rstd_h", [P, 32])
        minus_half = sb("minus_half", [P, 32])
        zeros = sb("zeros", [P, 512], mybir.dt.bfloat16)
        pos_i = sb("pos_i", [P, MT], I32)
        small = sb("small", [P, 256])
        ps = ctx.enter_context(nc.psum_tensor("ps", [P, 8, 512], F32))

        ident = const[:, C_IDENT:C_TRI]

        def acc(m):
            return ps[:, 2 * m:2 * m + 2, :].rearrange("p b n -> p (b n)")

        def bank(b):
            return ps[:, b, :]

        def region(a, *shape):
            n = int(np.prod(shape))
            names = "abcde"[:len(shape)]
            spec = f"p ({' '.join(names)}) -> p {' '.join(names)}"
            return arena[:, a:a + n].rearrange(spec, **dict(zip(names, shape)))

        def cut(ap, *shape):
            names = "abcde"[:len(shape)]
            spec = f"p ({' '.join(names)}) -> p {' '.join(names)}"
            return ap.rearrange(spec, **dict(zip(names, shape)))

        def over(ap, axis, n):
            v = ap.unsqueeze(axis)
            shape = list(v.shape)
            shape[axis] = n
            return v.to_broadcast(shape)

        def rows(w):
            return w.rearrange("(k p) n -> p k n", p=P)

        def dst(slot, k):
            return raw[:, slot, :].rearrange("p (k n) -> p k n", k=k)

        def halves(src, k):
            return [(src[:, i * k // 2:(i + 1) * k // 2, :],
                     lambda s, i=i: dst(s, k)[:, i * k // 2:(i + 1) * k // 2, :]) for i in range(2)]

        def ffn_up(l, which, half, j):
            w = T[f"ffn{which}_w_in"][l].rearrange("(k p) (u n) -> p k u n", p=P, u=2)
            return [(w[:, 4 * half:4 * half + 4, u, bass.ds(j * 256, 256)],
                     lambda s, u=u: raw[:, s, :].rearrange("p (k u n) -> p k u n", k=4, u=2)[:, :, u, :])
                    for u in range(2)]

        def wide(w, k0):
            return halves(rows(w)[:, bass.ds(k0, 2), :], 2)

        def block4(w, half, col):
            return halves(rows(w)[:, 4 * half:4 * half + 4, bass.ds(col, 512)], 4)

        def tall(w, col):
            return halves(rows(w)[:, :, bass.ds(col, 256)], 8)

        def ada_slab(run, i):
            return tall(T["ada_w_2"][run // 2], (run % 2) * 12 * 256 + i * 256)

        EVEN_CHUNKS = ((2048, 512), (2560, 256), (0, 512), (512, 512), (1024, 512), (1536, 512))

        junk = arena[:, 14336:15360]
        h1 = region(0, MT, 512)
        sg = region(1024, MT, 512)
        p_in = region(2048, MT, 256)
        gate_s = region(4096, MT, D)
        z_s = region(6144, MT, D)
        Ye = region(0, MT, EVEN_IN)
        rot = region(5632, MT, 10, 2, 32)
        kdup = region(6912, MT, 2, 2, 64)
        qT = region(7424, 4, SEQ)
        kT = region(8448, 2, SEQ)
        S1 = region(8960, 8, 256)
        S0 = region(11008, 8, 128)
        PT = region(12032, 6, 512)
        r1 = region(12032, MT, 10, 32)
        r2 = region(12672, MT, 10, 32)
        LF = region(5632, MT, 512)
        EB = region(6656, MT, 512)
        ENB = region(7680, MT, 512)
        ED = region(8704, MT, 512)
        lb_in = cut(table[:], 2, 512)
        lb, omlb = table[:, 0:512], table[:, 512:1024]
        states = region(9728, 3, 512)
        qsT = region(11776, 4, SEQ)
        ksT = region(12800, 4, SEQ)
        Yo = region(0, MT, ODD_IN)
        kTo = region(12288, 8, SEQ)
        qTo = cut(tmp[:], 8, SEQ)
        att_o = region(0, 4, 3, 128)
        gn_o = arena[:, 6144:6656]
        ropet = region(14336, 2, 4, 128)
        o_t = region(14336, 2, 512)
        t_buf = cut(tmp[:], KT, SEQ)
        dec = small[:, 0:16]
        mx = small[:, 16:32]
        nm = small[:, 32:48]
        es = small[:, 48:64]
        sm = small[:, 64:80]
        rd = small[:, 80:96]
        sink_b = small[:, 96:104]
        onorm_b = small[:, 128:256]
        ada_rows = sb("ada_rows", [4, 256])

        xn_lat = region(1024, MT, D)
        ones = arena[:, 3072:3200]
        diag = region(3200, KT, P)
        xn_ctx = region(4224, MT, D)
        out_t = region(4224, MT, D)
        relu_s = region(13312, MT, 512)
        PAD = 8
        A = region(6272, KT, SEQ + 2 * PAD)
        B = region(8448, KT, SEQ + 2 * PAD)
        C = region(10624, 6, SEQ + 2 * PAD)
        pool_w = region(12288, KT, 256)
        pooled = (region(1024, KT, SEQ), region(4224, KT, SEQ))
        inv_cnt = cut(table[:], 4, SEQ)
        YQK = region(4224, MT, 1536)
        YCK = region(7296, MT, 512)
        VL = region(0, MT, 512)
        VC = region(3200, MT, 512)
        xn_ctx_att = region(8320, MT, D)
        sq_l = region(10368, MT, 1536)
        sq_c = region(13440, MT, 512)
        rope_t = region(10368, 2, 12, 2, 32)
        kT_a = region(1024, 2, 4, SEQ)
        qT_a = cut(tmp[:], 8, SEQ)
        E = region(4224, 2, 4, 512)
        PT_a = region(8320, 2, 4, 4, P)
        OA = region(12416, MT, D)
        qk_g = cut(table[:, 0:256], 2, P)
        final_g = table[:]
        amx = small[:, 0:16]
        anm = small[:, 16:32]
        asm = small[:, 32:48]
        ard = small[:, 48:64]
        ATT_SCALE = 128 ** -0.5

        def scale_of(l, j, v):
            return mod[:, l, j, v, :]

        def ada_of(l, part, v):
            return ada_t[:, l * ADA_T + part * KT:l * ADA_T + (part + 1) * KT, v]

        block = ctx.enter_context(nc.Block())

        @block.sync
        def _(sp):
            sp.dma_start(h_lat[:], T["x"][0].rearrange("(m p) d -> p m d", p=P)).then_inc(S("x_in"), 16)
            sp.dma_start(const[:], T["const_tab"]).then_inc(S("const_in"), 16)
            a = tmp[:, 0:384].rearrange("p (j n) -> p j n", j=3)
            sp.dma_start(a[0:112, 0, :], T["norm_g"].rearrange("l n (k c) -> (l n k) c", c=P)).then_inc(S("vec_in"), 16)
            sp.dma_start(a[0:96, 1, :], T["ada_b_2"].rearrange("l (k c) -> (l k) c", c=P)).then_inc(S("vec_in"), 16)
            sp.dma_start(a[0:32, 2, :], T["norm_g_2"].rearrange("l n (k c) -> (l n k) c", c=P)).then_inc(S("vec_in"), 16)
            sp.dma_start(a[32:40, 2, :], T["c_2"].rearrange("b (k c) -> (b k) c", c=P)).then_inc(S("vec_in"), 16)
            sp.dma_start(a[40:48, 2, :], T["c_ctx_2"].rearrange("(k c) -> k c", c=P)).then_inc(S("vec_in"), 16)
            sp.dma_start(a[48:56, 2, :], T["pool_scale_2"].rearrange("b (k c) -> (b k) c", c=P)).then_inc(S("vec_in"), 16)
            sp.dma_start(pos_i[:], T["positions"][0].rearrange("(m p) -> p m", p=P),
                         allow_slow_non_contiguous=True).then_inc(S("pos_in"), 16)

            ring = Ring()

            def load(what):
                slot, uses = ring.take()
                if not isinstance(uses, int) or uses > 1:
                    sp.wait_ge(S(f"lo{slot}"), 2 * (uses - 1))
                for src, view in what:
                    sp.dma_start(view(slot), src).then_inc(S(f"raw{slot}"), 16)

            def ffn(run):
                l, which = run // 2, run % 2 + 1
                wo = T[f"ffn{which}_w_out"][l]

                def step(i):
                    load(ffn_up(l, which, 0, i + 1))
                    load(ffn_up(l, which, 1, i + 1))
                    load(wide(wo, 2 * i))
                    load(ada_slab(run, i + 1))

                load(ffn_up(l, which, 0, 0))
                load(ffn_up(l, which, 1, 0))
                load(ada_slab(run, 0))
                ring.loop(sp, FFN_STEPS - 1, 4, step)
                load(ada_slab(run, FFN_STEPS))
                load(wide(wo, 2 * FFN_STEPS - 2))

            def even():
                w = T["even_w_in"][0]
                for col, width in EVEN_CHUNKS:
                    if width == 256:
                        load(tall(w, col))
                    else:
                        load(block4(w, 0, col))
                        load(block4(w, 1, col))
                for j in range(4):
                    load(wide(T["even_w_out"][0], 2 * j))

            def ple(l):
                load(wide(T["ple_w_proj"][l], 0))
                for j in range(4):
                    load(wide(T["ple_w_gate"][l], 2 * j))

            def odd():
                def chunk(c, _):
                    for half in range(2):
                        load(block4(T["odd_w_in"][0], half, c * 512))

                ring.pairs(sp, ODD_IN // 512, chunk)
                for j in range(8):
                    load(wide(T["odd_w_out"][0], 2 * j))

            def mlp(l):
                w1, w2 = T["mlp_w1_2"][l], T["mlp_w2_2"][l]

                def step(i):
                    load(block4(w1, 0, (i + 1) * 512))
                    load(block4(w1, 1, (i + 1) * 512))
                    load(wide(w2, 4 * i))
                    load(wide(w2, 4 * i + 2))

                load(block4(w1, 0, 0))
                load(block4(w1, 1, 0))
                ring.loop(sp, MLP_STEPS - 1, 4, step)
                load(wide(w2, 4 * MLP_STEPS - 4))
                load(wide(w2, 4 * MLP_STEPS - 2))

            ffn(0)
            sp.dma_start(h_ctx[:], T["ctx_2"][0].rearrange("(m p) d -> p m d", p=P)).then_inc(S("ctx_in"), 16)
            even()
            ffn(1)
            ple(0)
            ffn(2)
            odd()
            ffn(3)
            ple(1)
            mlp(0)
            mlp(0)
            for c in (0, 1, 2, 3, 2, 3):
                for half in range(2):
                    load(block4(T["attn_w_qkv_2"][0], half, 512 * c))
            for j in range(4):
                load(wide(T["attn_w_o_2"][0], 2 * j))
            mlp(1)
            for m in range(MT):
                sp.wait_ge(S("out_ready"), m + 1)
                sp.dma_start(out[0, m * P:(m + 1) * P], out_t[:, m]).then_inc(S("stored"), 16)
            sp.wait_ge(S("stored"), 32)

        @block.tensor
        def _(pe):
            ring = Ring()
            n = {k: 0 for k in ("xt", "epi", "pj", "ada", "gain", "xn", "mlp")}

            def three(dst, a_hi, a_lo, slot, c0, width, start, stop):
                hi, lo = w_hi[:, slot, c0:c0 + width], w_lo[:, slot, c0:c0 + width]
                pe.matmul(dst, a_hi, hi, start=start, stop=False)
                pe.matmul(dst, a_hi, lo, start=False, stop=False)
                return pe.matmul(dst, a_lo, hi, start=False, stop=stop)

            def slab(slot, uses, half):
                pe.wait_ge(S(f"lo{slot}"), 2 * uses - 1 + half)

            def turn(dst, src, to=ident):
                k = src.shape[0]
                return pe.transpose(dst, src, to[0:k, 0:k])

            def xt_fill(src, order=(0, 1, 2, 3), of_h=False):
                for b in order:
                    if of_h and n["epi"] and b % 2 == 0:
                        pe.wait_ge(S("h_upd"), 4 * n["epi"] - 2 + b)
                    if b == 3 and n["ada"]:
                        pe.wait_ge(S("ada_cols"), n["ada"])
                    for k in range(2):
                        for m in range(MT):
                            c = (2 * b + k) * P
                            last = turn(ps[:, 4 + b, k * SEQ + m * P:k * SEQ + (m + 1) * P], src[:, m, c:c + P])
                    last.then_inc(S("xt_ps"), 1)
                    n["xt"] += 1

            def up(out0, sig0, wait_xt=False):
                for half in range(2):
                    slot, uses = ring.take()
                    if wait_xt:
                        pe.wait_ge(S("xt_ready"), n["xt"] - 2 + 2 * half)
                    for quarter in range(2):
                        slab(slot, uses, quarter)
                        for m in range(MT):
                            for t in (2 * quarter, 2 * quarter + 1):
                                k = 4 * half + t
                                last = three(bank(out0 + m), xt_hi[:, k, m * P:(m + 1) * P],
                                             xt_lo[:, k, m * P:(m + 1) * P],
                                             slot, t * 512, 512, k == 0, k == KT - 1)
                            if k == KT - 1 and m == 0:
                                last.then_inc(S(sig0), 1)
                        last.then_inc(S(f"used{slot}"), 1)

            def add_rows(a_hi, a_lo, k0, first, final, out0=0, sig0="acc0"):
                slot, uses = ring.take()
                for k in range(2):
                    slab(slot, uses, k)
                    for m in range(MT):
                        for h in range(2):
                            last = three(bank(out0 + 2 * m + h), a_hi[:, k0 + k, m * P:(m + 1) * P],
                                         a_lo[:, k0 + k, m * P:(m + 1) * P], slot, k * 1024 + h * 512, 512,
                                         first and k == 0, final and k == 1)
                        if final and k == 1 and m == 0:
                            last.then_inc(S(sig0), 1)
                    last.then_inc(S(f"used{slot}"), 1)

            def acc_is_free():
                if n["epi"]:
                    pe.wait_ge(S("acc_free"), 4 * n["epi"])

            def clear(b0):
                for b in range(b0, b0 + 4):
                    pe.matmul(bank(b), zeros[:, 0:P], zeros[:, :], start=True, stop=False)

            def hidden(tag, j, tiles):
                pe.wait_ge(S(tag + "h1"), 2 * j + 2)
                for b in range(tiles // 2):
                    for k in range(2):
                        for m in range(MT):
                            c = (2 * b + k) * P
                            last = turn(ps[:, 6 + b, k * SEQ + m * P:k * SEQ + (m + 1) * P], h1[:, m, c:c + P])
                    last.then_inc(S(tag + "ht_ps"), 1)

            def ada_product(j):
                if not isinstance(j, int) or j > 0:
                    pe.wait_ge(S("ada_cols"), j)
                slot, uses = ring.take()
                for k in range(KT):
                    if k % 4 == 0:
                        slab(slot, uses, k // 4)
                    for w in (w_hi, w_lo):
                        last = pe.matmul(ps[:, 7, 0:256], s4[:, k, :], w[:, slot, k * 256:(k + 1) * 256],
                                         start=k == 0 and w is w_hi, stop=k == KT - 1 and w is w_lo)
                    if k % 4 == 3:
                        last.then_inc(S(f"used{slot}"), 1)

            def ada_turn(j):
                pe.wait_ge(S("ada_row"), j + 1)
                for t in range(2):
                    last = pe.matmul(ps[:, 7, 256 + 2 * t:258 + 2 * t], ada_rows[0:4, t * P:(t + 1) * P],
                                     const[0:4, C_SEL:C_AX], start=True, stop=True)
                last.then_inc(S("ada_ps"), 1)

            def ffn(run):
                base = FFN_STEPS * run
                ada = (FFN_STEPS + 1) * run
                acc_is_free()
                clear(0)
                xt_fill(h_lat, of_h=True)
                up(4, "f_up0", wait_xt=True)
                if run == 0:
                    pe.wait_ge(S("s4_set"), 2)
                ada_product(ada)

                def step(i):
                    hidden("f_", base + i, 2)
                    up(4, "f_up0")
                    ada_turn(ada + i)
                    pe.wait_ge(S("f_ht"), base + i + 1)
                    add_rows(ht_hi, ht_lo, 0, False, False)
                    ada_product(ada + i + 1)

                ring.loop(pe, FFN_STEPS - 1, 4, step)
                hidden("f_", base + FFN_STEPS - 1, 2)
                ada_turn(ada + FFN_STEPS - 1)
                ada_product(ada + FFN_STEPS)
                pe.wait_ge(S("f_ht"), base + FFN_STEPS)
                add_rows(ht_hi, ht_lo, 0, False, True)
                ada_turn(ada + FFN_STEPS)
                n["epi"] += 1
                n["ada"] += FFN_STEPS + 1

            def chunk(c, wait_xt=False):
                if c >= 2:
                    pe.wait_ge(S("pj_act"), n["pj"] + c - 1)
                    pe.wait_ge(S("pj_dve"), n["pj"] + c - 1)
                up(4 + 2 * (c % 2), "pj0", wait_xt)

            pe.wait_ge(S("const_in"), 16)
            pe.wait_ge(S("vec_in"), 96)
            vec_rows = tmp[:, 0:384].rearrange("p (j n) -> p j n", j=3)
            for j, rows_j in enumerate((112, 96, 56)):
                turn(ps[:, j, 0:rows_j], vec_rows[0:rows_j, j, :]).then_inc(S("vec_ps"), 1)
            pe.wait_ge(S("x_in"), 16)
            pe.wait_ge(S("zeros_set"), 1)
            pe.wait_ge(S("vec_set"), 3)
            ffn(0)

            acc_is_free()
            xt_fill(h_lat, of_h=True)
            for c, (_, width) in enumerate(EVEN_CHUNKS):
                if width == 512:
                    chunk(c, wait_xt=c == 0)
                    continue
                slot, uses = ring.take()
                for half in range(2):
                    slab(slot, uses, half)
                    for m in range(MT):
                        for k in range(4 * half, 4 * half + 4):
                            last = three(ps[:, 6 + m, 0:256], xt_hi[:, k, m * P:(m + 1) * P],
                                         xt_lo[:, k, m * P:(m + 1) * P], slot, k * 256, 256, k == 0, k == KT - 1)
                        if half == 1 and m == 0:
                            last.then_inc(S("pj0"), 1)
                    last.then_inc(S(f"used{slot}"), 1)
            n["pj"] += 6
            pe.wait_ge(S("e_rope"), 1)
            for b in range(2):
                for k in range(2):
                    for m in range(MT):
                        q2 = rot[:, m, 4 * b + 2 * k:4 * b + 2 * k + 2].rearrange("p h x d -> p (h x d)")
                        last = turn(ps[:, b, k * SEQ + m * P:k * SEQ + (m + 1) * P], q2)
                last.then_inc(S("e_qk_ps"), 1)
            for g in range(2):
                for m in range(MT):
                    last = turn(ps[:, 2, g * SEQ + m * P:g * SEQ + (m + 1) * P],
                                kdup[:, m, g].rearrange("p u d -> p (u d)"))
            last.then_inc(S("e_qk_ps"), 1)
            pe.wait_ge(S("e_qT"), 2)
            pe.wait_ge(S("e_kT"), 1)
            pe.wait_ge(S("pj_act"), 6)
            pe.wait_ge(S("pj_dve"), 6)
            for o in range(2):
                q_rows = slice(64 * o, 64 * o + 64)
                for pair in range(4):
                    k_all = kT[q_rows, pair // 2, :]
                    pe.matmul(ps[:, 2 * o + pair // 2, (pair % 2) * 256:(pair % 2) * 256 + 256],
                              qT[q_rows, pair, P:2 * P], k_all, start=True, stop=True)
                    last = pe.matmul(ps[:, 4 + o, pair * P:(pair + 1) * P], qT[q_rows, pair, 0:P], k_all[:, 0:P],
                                     start=True, stop=True)
            last.then_inc(S("e_sc"), 1)
            pe.wait_ge(S("e_p"), 1)
            for b in range(6):
                for j in range(4):
                    if b < 2:
                        src = S0[:, 4 * b + j, :]
                    else:
                        src = S1[:, 2 * (b - 2) + j // 2, (j % 2) * P:(j % 2) * P + P]
                    last = turn(ps[:, b, j * P:(j + 1) * P], src)
                last.then_inc(S("e_pT"), 1)
            pe.wait_ge(S("e_PTa"), 3)
            pe.wait_ge(S("e_PTd"), 3)
            for pair in range(4):
                g = pair // 2
                for o in range(2):
                    to = ps[64 * o:64 * o + 64, 6 + pair // 2, (pair % 2) * SEQ:(pair % 2) * SEQ + SEQ]
                    v = [Ye[:, m, 2688 + 64 * g:2752 + 64 * g] for m in range(MT)]
                    pe.matmul(to[:, 0:P], v[0], PT[:, o, pair * P:(pair + 1) * P], start=True, stop=True)
                    i1 = 4 * o + pair
                    for half in range(2):
                        c = (i1 % 2) * 256 + half * P
                        last = pe.matmul(to[:, P:2 * P], v[half], PT[:, 2 + i1 // 2, c:c + P],
                                         start=half == 0, stop=half == 1)
                if pair % 2:
                    last.then_inc(S("xt_ps"), 1)
                    n["xt"] += 1
            pe.wait_ge(S("e_logf"), 1)
            for m in range(MT):
                pe.matmul(bank(m), const[:, C_TRI:C_SUF], LF[:, m, :], start=True, stop=True)
                pe.matmul(bank(2 + m), const[:, C_SUF:C_IND], LF[:, m, :], start=True, stop=True)
            for h in range(4):
                for m in range(MT):
                    last = pe.matmul(ps[:, 4, 4 * h + 2 * m:4 * h + 2 * m + 2], LF[:, m, h * P:(h + 1) * P],
                                     const[:, C_IND:C_SWA], start=True, stop=True)
            last.then_inc(S("e_sums"), 1)
            for which, sig, b0 in ((EB, "e_qs", 0), (ENB, "e_ks", 2)):
                pe.wait_ge(S(sig), 1)
                pe.wait_ge(S("e_eb"), 2 if b0 == 0 else 3)
                for b in range(2):
                    for k in range(2):
                        for m in range(MT):
                            h = 2 * b + k
                            last = turn(ps[:, b0 + b, k * SEQ + m * P:k * SEQ + (m + 1) * P], which[:, m, h * P:(h + 1) * P])
                    last.then_inc(S("e_qks_ps"), 1)
            pe.wait_ge(S("e_kd"), 1)
            pe.wait_ge(S("e_eb"), 4)
            pe.wait_ge(S("xt_ready"), n["xt"])
            for ch in range(3):
                m, r = ch // 2, slice(64 * (ch % 2), 64 * (ch % 2) + 64)
                for h in range(4):
                    last = pe.matmul(ps[:, 4 + ch, h * P:(h + 1) * P], ED[r, m, h * P:(h + 1) * P],
                                     Ye[r, m, 1024 + h * P:1024 + (h + 1) * P], start=True, stop=True)
            last.then_inc(S("e_kv"), 1)
            pe.wait_ge(S("e_qsT"), 2)
            pe.wait_ge(S("e_ksT"), 2)
            for m in range(MT):
                for h in range(4):
                    t = slice(m * P, (m + 1) * P)
                    last = pe.matmul(ps[:, m, h * P:(h + 1) * P], ksT[:, h, t], qsT[:, h, t], start=True, stop=True)
            last.then_inc(S("e_att"), 1)
            pe.wait_ge(S("e_state"), 1)
            pe.wait_ge(S("e_am"), 1)
            for m in range(MT):
                for h in range(4):
                    c = slice(h * P, (h + 1) * P)
                    pe.matmul(ps[:, 2 + m, c], LF[:, m, c], Ye[:, m, 1024 + h * P:1024 + (h + 1) * P],
                              start=True, stop=False, skip_group_check=True)
                    for j in range(2):
                        ch = 2 * m + j
                        if ch:
                            last = pe.matmul(ps[64 * j:64 * j + 64, 2 + m, c],
                                             qsT[:, h, ch * 64:ch * 64 + 64], states[:, ch - 1, c],
                                             start=False, stop=True, skip_group_check=True)
            last.then_inc(S("e_o"), 1)
            pe.wait_ge(S("e_oa"), 1)
            xt_fill(ENB, order=(0, 1))
            clear(0)
            pe.wait_ge(S("xt_ready"), n["xt"])
            for j in range(4):
                add_rows(xt_hi, xt_lo, 2 * j, False, j == 3)
            n["epi"] += 1

            def ple(l):
                acc_is_free()
                pe.wait_ge(S("p_in"), 16 * (l + 1))
                for k in range(2):
                    for m in range(MT):
                        last = turn(ps[:, 0, k * SEQ + m * P:k * SEQ + (m + 1) * P], p_in[:, m, k * P:(k + 1) * P])
                last.then_inc(S("pt_ps"), 1)
                xt_fill(h_lat, of_h=True)
                pe.wait_ge(S("pt_ready"), l + 1)
                clear(0)
                pe.wait_ge(S("xt_ready"), n["xt"])
                clear(4)
                add_rows(ht_hi, ht_lo, 0, False, True, out0=4, sig0="pr0")
                for j in range(4):
                    add_rows(xt_hi, xt_lo, 2 * j, False, j == 3)
                n["epi"] += 1

            ffn(1)
            ple(0)
            ffn(2)

            acc_is_free()
            xt_fill(h_lat, of_h=True)
            pe.wait_ge(S("xt_ready"), n["xt"])

            def odd_chunk(c, b):
                pe.wait_ge(S("pj_act"), c + n["pj"] - 1)
                pe.wait_ge(S("pj_dve"), c + n["pj"] - 1)
                up(b, "pj0")

            ring.pairs(pe, ODD_IN // 512, odd_chunk)
            n["pj"] += 12
            for m in range(MT):
                pe.wait_ge(S("o_rope"), 2 * (m + 1))
                pe.wait_ge(S("pj_act"), n["pj"])
                for b in range(4):
                    for j in range(4):
                        c = (4 * b + j) * P
                        last = turn(ps[:, 4 * (1 - m) + b, j * P:(j + 1) * P], Yo[:, m, c:c + P])
                    last.then_inc(S("o_qk_ps"), 1)
            pe.wait_ge(S("o_qT"), 4)
            pe.wait_ge(S("o_kT"), 4)
            for h in range(4):
                for kt in range(2):
                    pe.matmul(ps[:, h, 0:256], kTo[:, 2 * h + kt, 0:P], qTo[:, 2 * h + kt, :],
                              start=kt == 0, stop=kt == 1)
                for kt in range(2):
                    last = pe.matmul(ps[:, h, 256:384], kTo[:, 2 * h + kt, P:2 * P], qTo[:, 2 * h + kt, P:2 * P],
                                     start=kt == 0, stop=kt == 1)
                last.then_inc(S("o_sc"), 1)
            for h in range(4):
                pe.wait_ge(S("o_att"), h + 1)
                v = [Yo[:, m, 2048 + h * 512:2560 + h * 512] for m in range(MT)]
                b = (4, 6, 0, 2)[h]
                if h == 2:
                    pe.wait_ge(S("o_att"), 4)
                pe.matmul(bank(b), att_o[:, h, 0], v[0], start=True, stop=True).then_inc(S("o_o"), 1)
                pe.matmul(bank(b + 1), att_o[:, h, 1], v[0], start=True, stop=False)
                pe.matmul(bank(b + 1), att_o[:, h, 2], v[1], start=False, stop=True).then_inc(S("o_o"), 1)
            yo = Yo[:, :, 4096:6144]
            for part in range(2):
                pe.wait_ge(S("o_y"), 4 * (part + 1))
                if part == 0:
                    xt_fill(yo[:, :, 0:1024])
                    pe.wait_ge(S("o_y"), 8)
                    clear(0)
                else:
                    xt_fill(yo[:, :, 1024:2048])
                pe.wait_ge(S("xt_ready"), n["xt"])
                for j in range(4):
                    add_rows(xt_hi, xt_lo, 2 * j, False, part == 1 and j == 3)
            n["epi"] += 1

            ffn(3)
            ple(1)

            def wait_xn():
                n["xn"] += 1
                pe.wait_ge(S("xn_act"), n["xn"])
                pe.wait_ge(S("xn_dve"), n["xn"])

            def gain_row():
                acc_is_free()
                n["gain"] += 1
                pe.wait_ge(S("diag"), n["gain"])
                for b in range(2):
                    last = pe.matmul(bank(b), ones, diag[:, 4 * b:4 * b + 4].rearrange("p k c -> p (k c)"),
                                     start=True, stop=True)
                last.then_inc(S("gain_ps"), 1)

            def mlp(xn):
                base = MLP_STEPS * n["mlp"]
                n["mlp"] += 1
                wait_xn()
                xt_fill(xn, of_h=True)
                gain_row()
                up(4, "m_up0", wait_xt=True)
                pe.wait_ge(S("gain_set"), n["gain"])
                clear(0)

                def down(i, final):
                    pe.wait_ge(S("m_ht"), base + i + 1)
                    add_rows(ht_hi, ht_lo, 0, False, False)
                    add_rows(ht_hi, ht_lo, 2, False, final)

                def step(i):
                    hidden("m_", base + i, 4)
                    up(4, "m_up0")
                    down(i, False)

                ring.loop(pe, MLP_STEPS - 1, 4, step)
                hidden("m_", base + MLP_STEPS - 1, 4)
                down(MLP_STEPS - 1, True)
                n["epi"] += 1

            for v, xn in enumerate((xn_lat, xn_ctx)):
                wait_xn()
                if v:
                    pe.wait_ge(S("p_t"), 4)
                for b in range(4):
                    for k in range(2):
                        for m in range(MT):
                            c = (2 * b + k) * P
                            last = turn(ps[:, 4 + b, k * SEQ + m * P:k * SEQ + (m + 1) * P], xn[:, m, c:c + P])
                    last.then_inc(S("p_ps"), 1)
                if v == 0:
                    gain_row()
            for v in range(2):
                if v:
                    gain_row()
                pe.wait_ge(S("gain_set"), n["gain"])
                pe.wait_ge(S("pool_w_in"), 16)
                pe.wait_ge(S("pooled"), v + 1)
                for m in range(MT):
                    for kt in range(KT):
                        c = (kt // 2) * 256
                        last = pe.matmul(acc(m)[:, c:c + 256], pooled[v][:, kt, m * P:(m + 1) * P], pool_w[:, kt, :],
                                         start=kt % 2 == 0, stop=kt % 2 == 1)
                    last.then_inc(S("acc0" if m == 0 else "pool_y"), 1)
                n["epi"] += 1
            pe.wait_ge(S("p_t"), 8)
            mlp(xn_lat)
            mlp(xn_ctx)

            wait_xn()
            xt_fill(xn_lat, of_h=True)
            gain_row()
            for c in range(6):
                if c == 4:
                    pe.wait_ge(S("pj_act"), n["pj"] + 4)
                    pe.wait_ge(S("pj_dve"), n["pj"] + 4)
                    wait_xn()
                    xt_fill(xn_ctx_att)
                chunk(c, wait_xt=c in (0, 4))
            n["pj"] += 6
            pe.wait_ge(S("gain_set"), n["gain"])
            pe.wait_ge(S("a_rope"), 1)
            for b in range(4):
                for k in range(2):
                    for m in range(MT):
                        c = (2 * b + k) * P
                        last = turn(ps[:, b, k * SEQ + m * P:k * SEQ + (m + 1) * P], YQK[:, m, c:c + P])
                last.then_inc(S("a_q_ps"), 1)
            pe.wait_ge(S("pj_act"), n["pj"])
            pe.wait_ge(S("pj_dve"), n["pj"])
            pe.wait_ge(S("a_kc"), 1)
            for v, (src, c0) in enumerate(((YCK, 0), (YQK, 1024))):
                for g in range(4):
                    for m in range(MT):
                        c = c0 + g * P
                        at = (g % 2) * SEQ + m * P
                        last = turn(ps[:, 4 + 2 * v + g // 2, at:at + P], src[:, m, c:c + P])
                last.then_inc(S("a_k_ps"), 1)
            pe.wait_ge(S("a_qT"), 4)
            pe.wait_ge(S("a_kT"), 2)

            def scores(b):
                if b >= 2:
                    pe.wait_ge(S("a_oa"), b - 1)
                for j in range(4):
                    h = 4 * (b % 2) + j
                    q = qT_a[:, h, (b // 2) * P:(b // 2 + 1) * P]
                    for v in range(2):
                        last = pe.matmul(ps[:, h, v * SEQ:(v + 1) * SEQ], q, kT_a[:, v, h // 2, :],
                                         start=True, stop=True)
                last.then_inc(S("a_sc"), 1)

            def turn_weights(b):
                g0 = 4 * (b % 2)
                for j in range(4):
                    pe.wait_ge(S("a_e"), 4 * b + j + 1)
                    for k in range(4):
                        last = turn(ps[:, g0 + j, k * P:(k + 1) * P], E[:, b % 2, j, k * P:(k + 1) * P])
                    last.then_inc(S("a_pT"), 1)

            def weigh(b):
                g0 = 4 * (b % 2)
                pe.wait_ge(S("a_PTa"), 2 * b + 2)
                pe.wait_ge(S("a_PTd"), 2 * b + 2)
                for j in range(4):
                    c = ((g0 + j) // 2) * P
                    for k in range(4):
                        val = (VC, VL)[k // 2][:, k % 2, c:c + P]
                        last = pe.matmul(ps[:, g0, j * P:(j + 1) * P], PT_a[:, b % 2, j, k, :], val,
                                         start=k == 0, stop=k == 3)
                last.then_inc(S("a_o"), 1)

            for b in (0, 2):
                for part in (scores, turn_weights, weigh):
                    part(b)
                    part(b + 1)
            pe.wait_ge(S("a_oa"), 4)
            xt_fill(OA)
            clear(0)
            pe.wait_ge(S("xt_ready"), n["xt"])
            for j in range(4):
                add_rows(xt_hi, xt_lo, 2 * j, False, j == 3)
            n["epi"] += 1
            mlp(xn_lat)

        @block.scalar
        def _(act):
            ring = Ring()
            n = {k: 0 for k in ("xt", "sq", "epi", "pj", "gain", "mlp")}

            def split():
                slot, uses = ring.take()
                act.wait_ge(S(f"raw{slot}"), 32 * uses)
                for half in range(2):
                    if not isinstance(uses, int) or uses > 1:
                        act.wait_ge(S(f"used{slot}"), 2 * uses - 3 + half)
                    c = slice(half * 1024, half * 1024 + 1024)
                    act.activation(w_hi[:, slot, c], raw[:, slot, c], ACT.Copy).then_inc(S(f"hi{slot}"), 1)

            def xt_turn(scale=None, bias=None, order=(0, 1, 2, 3)):
                for b in order:
                    act.wait_ge(S("xt_ps"), n["xt"] + 1)
                    n["xt"] += 1
                    if scale is None:
                        last = act.activation(t_buf[:, 2 * b:2 * b + 2, :], cut(bank(4 + b), 2, SEQ), ACT.Copy)
                    else:
                        for k in range(2):
                            kt = 2 * b + k
                            last = act.activation(t_buf[:, kt, :], ps[:, 4 + b, k * SEQ:(k + 1) * SEQ], ACT.Identity,
                                                  bias=0.0 if bias is None else bias[:, kt:kt + 1],
                                                  scale=scale[:, kt:kt + 1])
                    last.then_inc(S("xt_t"), 1)

            def squares(src, scale=1.0):
                for m in range(MT):
                    if n["sq"] or m:
                        act.wait_ge(S("ssq"), 2 * n["sq"] + m)
                    act.activation(junk, src(m), ACT.Square, scale=scale,
                                   accum_out=ssq[:, n["sq"] % 4, m:m + 1]).then_inc(S("ssq"), 1)
                n["sq"] += 1

            def wait_used(k):
                slot, uses = ring.back(k)
                act.wait_ge(S(f"used{slot}"), 2 * uses)

            def acc_when_done(m):
                if m == 0:
                    act.wait_ge(S("acc0"), n["epi"] + 1)
                else:
                    wait_used(3)
                return acc(m)

            def gain_of(l, j):
                c = (l * N_NORMS + j) * KT
                return norm_t[:, c:c + KT]

            def ada_row():
                act.activation(ada_rows[:, :], ps[0:4, 7, 0:256], ACT.Copy).then_inc(S("ada_row"), 1)

            def ffn(run):
                base = FFN_STEPS * run
                l = run // 2
                k = n["sq"] % 4
                xt_turn(gain_of(l, 4 * (run % 2)))
                if run == 0:
                    split()
                    split()
                split()
                squares(lambda m: h_lat[:, m, :])

                def swish(j, k_back):
                    for m in range(MT):
                        if m == 0:
                            act.wait_ge(S("f_up0"), j + 1)
                        else:
                            wait_used(k_back)
                        act.activation(sg[:, m, 0:256], ps[:, 4 + m, 0:256], ACT.Silu,
                                       scale=rstd[:, k, m:m + 1]).then_inc(S("f_sg"), 1)

                def turned(j):
                    act.wait_ge(S("f_ht_ps"), j + 1)
                    act.activation(ht_hi[:, 0:2, :], cut(bank(6), 2, SEQ), ACT.Copy).then_inc(S("f_ht_hi"), 1)
                    wait_used(3)
                    ada_row()

                act.wait_ge(S("rstd"), n["sq"])
                swish(base, 2)
                split()
                split()

                def step(i):
                    turned(base + i)
                    split()
                    split()
                    swish(base + i + 1, 3)
                    split()
                    split()

                ring.loop(act, FFN_STEPS - 1, 4, step)
                turned(base + FFN_STEPS - 1)
                split()
                wait_used(3)
                ada_row()
                split()
                squares(acc_when_done)
                n["epi"] += 1

            act.wait_ge(S("vec_set"), 3)
            act.activation(small[:, 0:16], vec_t[:, 32:48], ACT.Silu).then_inc(S("silu_c"), 1)
            ffn(0)

            act.wait_ge(S("rope_ang"), 1)
            act.activation(rope_cos[:], rope_cos[:], ACT.Sin).then_inc(S("rope_set"), 1)
            act.activation(rope_sin[:], rope_sin[:], ACT.Sin).then_inc(S("rope_set"), 1)
            xt_turn(gain_of(0, 2))
            split()
            k = n["sq"] % 4
            squares(lambda m: h_lat[:, m, :])
            act.wait_ge(S("rstd"), n["sq"])
            for c, (col, width) in enumerate(EVEN_CHUNKS):
                if width == 512:
                    split()
                act.wait_ge(S("pj0"), n["pj"] + c + 1)
                act.activation(Ye[:, 0, col:col + width], ps[:, 4 + 2 * (c % 2), 0:width], ACT.Copy,
                               scale=rstd[:, k, 0:1]).then_inc(S("pj_act"), 1)
                split()
            n["pj"] += 6
            for b in range(2):
                act.wait_ge(S("e_qk_ps"), b + 1)
                act.activation(qT[:, 2 * b:2 * b + 2, :], cut(bank(b), 2, SEQ), ACT.Copy).then_inc(S("e_qT"), 1)
            act.wait_ge(S("pj_act"), n["pj"])
            act.wait_ge(S("pj_dve"), n["pj"])
            act.activation(Ye[:, :, 0:512], Ye[:, :, 0:512], ACT.Silu).then_inc(S("e_silu"), 1)
            act.activation(Ye[:, :, 1536:2048], Ye[:, :, 1536:2048], ACT.Silu).then_inc(S("e_silu"), 1)
            act.activation(Ye[:, :, 512:1024], Ye[:, :, 512:1024], ACT.Tanh, scale=0.5).then_inc(S("e_silu"), 1)
            act.wait_ge(S("e_lb_in"), 1)
            act.activation(lb_in, lb_in, ACT.Exp).then_inc(S("e_lb_exp"), 1)
            act.wait_ge(S("e_mx"), 1)
            for i in range(8):
                for blk, buf in ((0, S0), (1, S1)):
                    c = blk * 8 + i
                    act.activation(buf[:, i, :], buf[:, i, :], ACT.Exp, bias=nm[:, c:c + 1],
                                   accum_out=sm[:, c:c + 1])
            act.activation(es, es, ACT.Exp).then_inc(S("e_exp"), 1)
            for b in range(0, 6, 2):
                act.wait_ge(S("e_pT"), b + 1)
                act.activation(PT[:, b, :], bank(b), ACT.Copy).then_inc(S("e_PTa"), 1)
            xt_turn(order=(2, 3))
            act.wait_ge(S("e_f"), 1)
            act.activation(LF, LF, ACT.Ln).then_inc(S("e_logf"), 1)
            act.wait_ge(S("e_sums"), 1)
            act.activation(EB, ps[:, 0:2, :], ACT.Exp).then_inc(S("e_eb"), 1)
            act.activation(ENB, ps[:, 0:2, :], ACT.Exp, scale=-1.0).then_inc(S("e_eb"), 1)
            act.activation(ED, ps[:, 2:4, :], ACT.Exp).then_inc(S("e_eb"), 1)
            act.activation(dec, ps[:, 4, 0:16], ACT.Exp).then_inc(S("e_eb"), 1)
            for b in range(2):
                act.wait_ge(S("e_qks_ps"), b + 1)
                act.activation(qsT[:, 2 * b:2 * b + 2, :], cut(bank(b), 2, SEQ), ACT.Copy).then_inc(S("e_qsT"), 1)
            act.wait_ge(S("e_o"), 1)
            act.activation(EB, ps[:, 2:4, :], ACT.Square).then_inc(S("e_osq"), 1)
            xt_turn(order=(0, 1))
            for _ in range(3):
                split()
            squares(acc_when_done)
            n["epi"] += 1

            def ple(l):
                act.wait_ge(S("pt_ps"), l + 1)
                act.activation(ht_hi[:, 0:2, :], cut(bank(0), 2, SEQ), ACT.Copy).then_inc(S("pt_hi"), 1)
                xt_turn()
                for _ in range(5):
                    split()
                for m in range(MT):
                    if m == 0:
                        act.wait_ge(S("acc0"), n["epi"] + 1)
                    else:
                        wait_used(3)
                    act.activation(gate_s[:, m, :], acc(m), ACT.Tanh, scale=0.5).then_inc(S("acc_free"), 2)

                def z_when_done(m):
                    act.wait_ge(S("z_ready"), 2 * l + m + 1)
                    return z_s[:, m, :]
                squares(z_when_done, scale=0.5)
                n["epi"] += 1

            ffn(1)
            ple(0)
            ffn(2)

            xt_turn(gain_of(1, 2))
            split()
            k = n["sq"] % 4
            squares(lambda m: h_lat[:, m, :])
            act.wait_ge(S("rstd"), n["sq"])

            def odd_chunk(c, b):
                split()
                act.wait_ge(S("pj0"), c + n["pj"] + 1)
                act.activation(Yo[:, 0, bass.ds(c * 512, 512)], bank(b), ACT.Copy,
                               scale=rstd[:, k, 0:1]).then_inc(S("pj_act"), 1)
                split()

            ring.pairs(act, ODD_IN // 512, odd_chunk)
            n["pj"] += 12
            act.wait_ge(S("pj_dve"), n["pj"])
            act.wait_ge(S("pj_act"), n["pj"])
            for m in range(MT):
                act.activation(Yo[:, m, 4096:6144], Yo[:, m, 4096:6144], ACT.Silu).then_inc(S("o_silu"), 1)
            for m in range(MT):
                for b in range(2):
                    act.wait_ge(S("o_qk_ps"), 4 * m + b + 1)
                    act.activation(qTo[:, 4 * b:4 * b + 4, m * P:(m + 1) * P],
                                   cut(bank(4 * (1 - m) + b), 4, P), ACT.Copy).then_inc(S("o_qT"), 1)
            for h in range(4):
                for m in range(MT):
                    act.wait_ge(S("o_o"), 2 * h + m + 1)
                    i = 2 * h + m
                    if i >= 4:
                        act.wait_ge(S("o_ssq"), i - 3)
                    act.activation(cut(tmp[:], 4, 512)[:, i % 4], bank((4, 6, 0, 2)[h] + m), ACT.Square,
                                   accum_out=ssq_h[:, 8 + 2 * h + m:9 + 2 * h + m]).then_inc(S("o_ssq"), 1)
            act.wait_ge(S("o_ssq"), 8)
            for part in range(2):
                xt_turn()
                for _ in range(3 if part == 0 else 4):
                    split()
            squares(acc_when_done)
            n["epi"] += 1

            ffn(3)
            ple(1)

            def norm(h, epilogues, xn):
                act.wait_ge(S("h_upd"), 4 * epilogues)
                k = n["sq"] % 4
                squares(lambda m: h[:, m, :])
                act.wait_ge(S("rstd"), n["sq"])
                act.activation(xn[:, 0, :], h[:, 0, :], ACT.Copy, scale=rstd[:, k, 0:1]).then_inc(S("xn_act"), 1)

            def gain_copy():
                n["gain"] += 1
                act.wait_ge(S("gain_ps"), n["gain"])
                act.activation(gain[:], acc(0), ACT.Copy).then_inc(S("gain_set"), 1)

            def mlp(l, v, ahead=None, last=False):
                base = MLP_STEPS * n["mlp"]
                n["mlp"] += 1
                xt_turn(scale_of(l, 1, v), ada_of(l, 3, v))
                gain_copy()
                split()
                if ahead:
                    norm(*ahead)

                def turned(j):
                    act.wait_ge(S("m_ht_ps"), 2 * j + 2)
                    act.activation(ht_hi[:], cut(ps[:, 6:8, :].rearrange("p b n -> p (b n)"), 4, SEQ),
                                   ACT.Copy).then_inc(S("m_ht_hi"), 1)

                def relu(j, k_back):
                    for m in range(MT):
                        if m == 0:
                            act.wait_ge(S("m_up0"), j + 1)
                        else:
                            wait_used(k_back)
                        act.activation(relu_s[:, m, :], bank(4 + m), ACT.Relu).then_inc(S("m_relu"), 1)

                def step(i):
                    turned(base + i)
                    split()
                    split()
                    relu(base + i + 1, 3)
                    split()
                    split()

                relu(base, 2)
                split()
                ring.loop(act, MLP_STEPS - 1, 4, step)
                turned(base + MLP_STEPS - 1)
                if not last:
                    split()
                    split()
                n["epi"] += 1

            norm(h_lat, 8, xn_lat)
            act.wait_ge(S("ctx_in"), 16)
            norm(h_ctx, 8, xn_ctx)
            act.wait_ge(S("pads"), 1)
            for v in range(2):
                if v:
                    act.wait_ge(S("pooled"), v)
                for b in range(4):
                    act.wait_ge(S("p_ps"), 4 * v + b + 1)
                    for k in range(2):
                        kt = 2 * b + k
                        last = act.activation(A[:, kt, PAD:PAD + SEQ], ps[:, 4 + b, k * SEQ:(k + 1) * SEQ],
                                              ACT.Identity, bias=ada_of(0, 0, v)[:, kt:kt + 1],
                                              scale=scale_of(0, 0, v)[:, kt:kt + 1])
                    last.then_inc(S("p_t"), 1)
                gain_copy()
                n["epi"] += 1
            norm(h_lat, 9, xn_lat)
            mlp(0, 0, ahead=(h_ctx, 10, xn_ctx))
            mlp(0, 1, ahead=(h_lat, 11, xn_lat))

            xt_turn(scale_of(1, 0, 0), ada_of(1, 0, 0))
            gain_copy()
            split()
            norm(h_ctx, 12, xn_ctx_att)
            to = [YQK[:, 0, 0:512], YQK[:, 0, 512:1024], YQK[:, 0, 1024:1536], VL[:, 0], YCK[:, 0], VC[:, 0]]
            for c in range(6):
                if c == 4:
                    xt_turn(scale_of(1, 0, 1), ada_of(1, 0, 1))
                    act.wait_ge(S("pj_dve"), n["pj"] + 4)
                    act.wait_ge(S("pj_act"), n["pj"] + 4)
                    act.activation(sq_l, YQK, ACT.Square).then_inc(S("a_sq"), 1)
                if c == 5:
                    act.wait_ge(S("pj_dve"), n["pj"] + 5)
                    act.wait_ge(S("pj_act"), n["pj"] + 5)
                    act.activation(sq_c, YCK, ACT.Square).then_inc(S("a_sq"), 1)
                split()
                act.wait_ge(S("pj0"), n["pj"] + c + 1)
                act.activation(to[c], bank(4 + 2 * (c % 2)), ACT.Copy).then_inc(S("pj_act"), 1)
                split()
            n["pj"] += 6
            for b in range(2):
                act.wait_ge(S("a_q_ps"), b + 1)
                act.activation(qT_a[:, 2 * b:2 * b + 2, :], cut(bank(b), 2, SEQ), ACT.Copy).then_inc(S("a_qT"), 1)
            act.wait_ge(S("a_k_ps"), 1)
            act.activation(kT_a[:, 0], cut(ps[:, 4:6, :].rearrange("p b n -> p (b n)"), 4, SEQ),
                           ACT.Copy).then_inc(S("a_kT"), 1)

            def exps(b):
                act.wait_ge(S("a_mx"), b + 1)
                for j in range(4):
                    c = 4 * b + j
                    act.activation(E[:, b % 2, j, :], bank(4 * (b % 2) + j), ACT.Exp, bias=anm[:, c:c + 1],
                                   scale=ATT_SCALE, accum_out=asm[:, c:c + 1]).then_inc(S("a_e"), 1)

            def turned_weights(b):
                for j in (0, 2):
                    act.wait_ge(S("a_pT"), 4 * b + j + 1)
                    act.activation(PT_a[:, b % 2, j], cut(bank(4 * (b % 2) + j), 4, P),
                                   ACT.Copy).then_inc(S("a_PTa"), 1)

            for b in (0, 2):
                for part in (exps, turned_weights):
                    part(b)
                    part(b + 1)
            xt_turn()
            for _ in range(3):
                split()
            n["epi"] += 1
            norm(h_lat, 13, xn_lat)
            mlp(1, 0, last=True)
            act.wait_ge(S("h_upd"), 4 * 14)
            squares(lambda m: h_lat[:, m, :])

        @block.vector
        def _(dve):
            ring = Ring()
            n = {k: 0 for k in ("xt", "sq", "epi", "pj", "ple", "step", "gain", "mlp")}
            TT = dve.tensor_tensor

            def step(ins):
                n["step"] += 1
                ins.then_inc(S("dve_step"), 1)
                dve.wait_ge(S("dve_step"), n["step"])

            def split():
                slot, uses = ring.take()
                for half in range(2):
                    c = slice(half * 1024, half * 1024 + 1024)
                    dve.wait_ge(S(f"hi{slot}"), 2 * uses - 1 + half)
                    TT(w_lo[:, slot, c], raw[:, slot, c], w_hi[:, slot, c].bitcast(F32),
                       ALU.subtract).then_inc(S(f"lo{slot}"), 1)

            def xt_split(order=(0, 1, 2, 3)):
                for b in order:
                    dve.wait_ge(S("xt_t"), n["xt"] + 1)
                    n["xt"] += 1
                    kk = slice(2 * b, 2 * b + 2)
                    step(dve.tensor_copy(xt_hi[:, kk, :], t_buf[:, kk, :]))
                    TT(xt_lo[:, kk, :], t_buf[:, kk, :], xt_hi[:, kk, :].bitcast(F32),
                       ALU.subtract).then_inc(S("xt_ready"), 1)

            def epilogue(src, scaled=True, target=None):
                target = h_lat if target is None else target
                k = n["sq"] % 4
                n["sq"] += 1
                dve.wait_ge(S("rstd"), n["sq"])
                dve.wait_ge(S("gain_in"), 16 * (n["epi"] + 1))
                for half in range(2):
                    c = slice(512 * half, 512 * half + 512)
                    for m in range(MT):
                        ins = dve.scalar_tensor_tensor(cut(tmp[:], 2, MT, 512)[:, half, m], src(m)[:, c], rstd[:, k, m:m + 1],
                                                       gain[:, c], ALU.mult, ALU.mult)
                        if scaled:
                            ins.then_inc(S("acc_free"), 1)
                        else:
                            ins.then_inc(S("z_used"), 1)
                    if scaled:
                        dve.wait_ge(S("acc_free"), 4 * n["epi"] + 2 * half + 2)
                    else:
                        dve.wait_ge(S("z_used"), 4 * n["ple"] + 2 * half + 2)
                    for m in range(MT):
                        TT(target[:, m, c], target[:, m, c], cut(tmp[:], 2, MT, 512)[:, half, m],
                           ALU.add).then_inc(S("h_upd"), 1)
                n["epi"] += 1

            def ada_cols(at):
                dst = ada_t[:, bass.ds(at, 2), :] if not isinstance(at, int) else ada_t[:, at:at + 2, :]
                dve.tensor_copy(dst, cut(ps[:, 7, 256:260], 2, 2)).then_inc(S("ada_cols"), 1)

            def ffn(run):
                base = FFN_STEPS * run
                ada = (FFN_STEPS + 1) * run
                k = n["sq"] % 4
                xt_split()
                if run == 0:
                    split()
                    split()
                split()
                n["sq"] += 1

                def gated(j):
                    for m in range(MT):
                        dve.wait_ge(S("f_sg"), 2 * j + m + 1)
                        dve.scalar_tensor_tensor(h1[:, m, 0:256], ps[:, 4 + m, 256:512], rstd[:, k, m:m + 1],
                                                 sg[:, m, 0:256], ALU.mult, ALU.mult).then_inc(S("f_h1"), 1)

                def ht_low(j):
                    dve.wait_ge(S("f_ht_hi"), j + 1)
                    TT(ht_lo[:, 0:2, :], cut(bank(6), 2, SEQ), ht_hi[:, 0:2, :].bitcast(F32),
                       ALU.subtract).then_inc(S("f_ht"), 1)

                def step(i):
                    ht_low(base + i)
                    split()
                    dve.wait_ge(S("ada_ps"), ada + i + 1)
                    ada_cols(2 * ada + 2 * i)
                    split()
                    gated(base + i + 1)
                    split()
                    split()

                gated(base)
                split()
                split()
                ring.loop(dve, FFN_STEPS - 1, 4, step)
                ht_low(base + FFN_STEPS - 1)
                dve.wait_ge(S("ada_ps"), ada + FFN_STEPS)
                ada_cols(2 * (ada + FFN_STEPS - 1))
                split()
                split()
                dve.wait_ge(S("ada_ps"), ada + FFN_STEPS + 1)
                ada_cols(2 * (ada + FFN_STEPS))
                epilogue(acc)

            dve.memset(zeros[:], 0.0).then_inc(S("zeros_set"), 1)
            for j, (dst, w) in enumerate(((norm_t, 112), (adab_t, 96), (vec_t, 56))):
                dve.wait_ge(S("vec_ps"), j + 1)
                dve.tensor_copy(dst[:], ps[:, j, 0:w]).then_inc(S("vec_set"), 1)
            dve.wait_ge(S("silu_c"), 1)
            dve.wait_ge(S("s4_zero"), 1)
            sil = small[:, 0:16].rearrange("p (v k) -> p k v", v=2)
            dve.tensor_copy(s4[:, :, 0:2], sil).then_inc(S("s4_set"), 1)
            dve.wait_ge(S("s4_set"), 1)
            TT(s4[:, :, 2:4], sil, s4[:, :, 0:2].bitcast(F32), ALU.subtract).then_inc(S("s4_set"), 1)
            ffn(0)

            xt_split()
            split()
            k = n["sq"] % 4
            n["sq"] += 1
            def rope_even():
                dve.wait_ge(S("pj_act"), n["pj"] + 2)
                dve.wait_ge(S("pj_dve"), n["pj"] + 2)
                dve.wait_ge(S("rope_set"), 2)
                qk = Ye[:, :, 2048:2688].rearrange("p m (h x d) -> p m h x d", h=10, x=2)
                x1, x2 = qk[:, :, :, 0, :], qk[:, :, :, 1, :]
                cos, sin = over(rope_cos[:, :, 0:32], 2, 10), over(rope_sin[:, :, 0:32], 2, 10)
                TT(rot[:, :, :, 0, :], x1, cos, ALU.mult)
                TT(r1, x2, sin, ALU.mult)
                TT(rot[:, :, :, 1, :], x2, cos, ALU.mult)
                step(TT(r2, x1, sin, ALU.mult))
                TT(rot[:, :, :, 0, :], rot[:, :, :, 0, :], r1, ALU.subtract)
                step(TT(rot[:, :, :, 1, :], rot[:, :, :, 1, :], r2, ALU.add))
                krot = rot[:, :, 8:10].rearrange("p m g x d -> p m g (x d)")
                dve.tensor_copy(kdup[:, :, :, 0, :], krot)
                dve.tensor_copy(kdup[:, :, :, 1, :], krot).then_inc(S("e_rope"), 1)

            for c, (col, width) in enumerate(EVEN_CHUNKS):
                if width == 512:
                    split()
                if c == 0:
                    dve.wait_ge(S("rstd"), n["sq"])
                slot, uses = ring.back(3)
                dve.wait_ge(S(f"used{slot}"), 2 * uses)
                dve.tensor_scalar(Ye[:, 1, col:col + width], ps[:, 5 + 2 * (c % 2), 0:width], rstd[:, k, 1:2], None,
                                  ALU.mult).then_inc(S("pj_dve"), 1)
                split()
                if c == 3:
                    rope_even()
            n["pj"] += 6
            dve.wait_ge(S("lb_in"), 16)
            top = tmp[:, 0:512]
            step(TT(top, lb_in[:, 0], lb_in[:, 1], ALU.max))
            TT(lb_in, lb_in, over(top, 1, 2), ALU.subtract).then_inc(S("e_lb_in"), 1)
            dve.wait_ge(S("e_qk_ps"), 3)
            dve.tensor_copy(kT, cut(bank(2), 2, SEQ)).then_inc(S("e_kT"), 1)
            dve.wait_ge(S("e_sc"), 1)
            mask = const[:, C_SWA:C_INV]
            for o in range(2):
                dve.scalar_tensor_tensor(S1[:, 4 * o:4 * o + 4, :],
                                         cut(ps[:, 2 * o:2 * o + 2, :].rearrange("p b n -> p (b n)"), 4, 256),
                                         0.125, over(mask, 1, 4), ALU.mult, ALU.add)
                last = dve.scalar_tensor_tensor(S0[:, 4 * o:4 * o + 4, :], cut(bank(4 + o), 4, P), 0.125,
                                                over(mask[:, P:256], 1, 4), ALU.mult, ALU.add)
            step(last)
            dve.tensor_reduce(mx[:, 0:8], S0, AX_X, ALU.max)
            step(dve.tensor_reduce(mx[:, 8:16], S1, AX_X, ALU.max))
            dve.wait_ge(S("sink_in"), 32)
            sinks = over(sink_b, 1, 2)
            step(TT(cut(mx, 2, 8), cut(mx, 2, 8), sinks, ALU.max))
            step(dve.tensor_scalar(nm, mx, -1.0, None, ALU.mult))
            TT(cut(es, 2, 8), cut(nm, 2, 8), sinks, ALU.add).then_inc(S("e_mx"), 1)
            dve.wait_ge(S("e_lb_exp"), 1)
            step(TT(top, lb_in[:, 0], lb_in[:, 1], ALU.add))
            step(dve.reciprocal(top, top))
            step(TT(lb, lb_in[:, 0], top, ALU.mult))
            step(dve.tensor_scalar(omlb, lb, -1.0, 1.0, ALU.mult, ALU.add))
            dve.wait_ge(S("e_exp"), 1)
            step(TT(rd, sm, es, ALU.add))
            step(dve.reciprocal(rd, rd))
            TT(S0, S0, rd[:, 0:8].unsqueeze(2).to_broadcast([P, 8, P]), ALU.mult)
            TT(S1, S1, rd[:, 8:16].unsqueeze(2).to_broadcast([P, 8, 256]), ALU.mult).then_inc(S("e_p"), 1)
            for b in range(1, 6, 2):
                dve.wait_ge(S("e_pT"), b + 1)
                dve.tensor_copy(PT[:, b, :], bank(b)).then_inc(S("e_PTd"), 1)
            xt_split(order=(2, 3))
            dve.wait_ge(S("e_silu"), 3)
            fk = Ye[:, :, 512:1024]
            step(dve.tensor_scalar(LF, fk, 0.5, 0.5, ALU.mult, ALU.add))
            step(TT(LF, LF, over(omlb, 1, 2), ALU.mult))
            step(TT(LF, LF, over(lb, 1, 2), ALU.add))
            dve.tensor_scalar(fk, LF, -1.0, 1.0, ALU.mult, ALU.add).then_inc(S("e_f"), 1)
            dve.wait_ge(S("e_f"), 1)
            dve.wait_ge(S("e_eb"), 1)
            TT(EB, EB, Ye[:, :, 0:512], ALU.mult).then_inc(S("e_qs"), 1)
            dve.wait_ge(S("e_eb"), 2)
            TT(ENB, ENB, fk, ALU.mult).then_inc(S("e_ks"), 1)
            dve.wait_ge(S("e_eb"), 3)
            TT(ED, ED, fk, ALU.mult).then_inc(S("e_kd"), 1)
            for b in range(2):
                dve.wait_ge(S("e_qks_ps"), 3 + b)
                dve.tensor_copy(ksT[:, 2 * b:2 * b + 2, :], cut(bank(2 + b), 2, SEQ)).then_inc(S("e_ksT"), 1)
            dve.wait_ge(S("e_eb"), 4)
            dve.wait_ge(S("e_kv"), 1)
            step(dve.tensor_copy(states[:, 0], bank(4)))
            for ch in range(1, 3):
                for h in range(4):
                    c = slice(h * P, (h + 1) * P)
                    ins = dve.scalar_tensor_tensor(states[:, ch, c], states[:, ch - 1, c],
                                                   dec[:, 4 * h + ch:4 * h + ch + 1], ps[:, 4 + ch, c],
                                                   ALU.mult, ALU.add)
                if ch == 1:
                    step(ins)
            ins.then_inc(S("e_state"), 1)
            dve.wait_ge(S("e_att"), 1)
            step(dve.tensor_scalar(LF, ps[:, 0:2, :], 3.0e38, -3.0e38, ALU.min, ALU.max))
            tri = over(const[:, C_TRI:C_SUF], 1, 8)
            att8 = LF.rearrange("p m (h c) -> p (m h) c", h=4)
            TT(att8, att8, tri, ALU.mult).then_inc(S("e_am"), 1)
            dve.wait_ge(S("e_osq"), 1)
            dve.tensor_reduce(ssq_h[:, 0:8], EB.rearrange("p m (h c) -> p (m h) c", h=4), AX_X,
                              ALU.add).then_inc(S("ssq_h"), 1)
            dve.wait_ge(S("rstd_h"), 1)
            o8 = ENB.rearrange("p m (h c) -> p (m h) c", h=4)
            step(TT(o8, ps[:, 2:4, :].rearrange("p b (h c) -> p (b h) c", h=4),
                    rstd_h[:, 0:8].unsqueeze(2).to_broadcast([P, 8, P]), ALU.mult))
            dve.wait_ge(S("onorm_in"), 16)
            step(TT(o8, o8, over(onorm_b, 1, 8), ALU.mult))
            TT(ENB, ENB, Ye[:, :, 1536:2048], ALU.mult).then_inc(S("e_oa"), 1)
            xt_split(order=(0, 1))
            for _ in range(3):
                split()
            epilogue(acc)

            def ple(l):
                dve.wait_ge(S("pt_hi"), l + 1)
                TT(ht_lo[:, 0:2, :], cut(bank(0), 2, SEQ), ht_hi[:, 0:2, :].bitcast(F32),
                   ALU.subtract).then_inc(S("pt_ready"), 1)
                xt_split()
                for _ in range(5):
                    split()
                for m in range(MT):
                    dve.wait_ge(S("acc_free"), 4 * n["epi"] + 2 * m + 2)
                    proj = ps[:, 4 + 2 * m:6 + 2 * m, :].rearrange("p b n -> p (b n)")
                    dve.scalar_tensor_tensor(z_s[:, m, :], gate_s[:, m, :], 1.0, proj, ALU.add,
                                             ALU.mult).then_inc(S("z_ready"), 1)
                dve.wait_ge(S("z_ready"), 2 * (l + 1))
                epilogue(lambda m: z_s[:, m, :], scaled=False)
                n["ple"] += 1

            ffn(1)
            ple(0)
            ffn(2)

            xt_split()
            split()
            k = n["sq"] % 4
            n["sq"] += 1
            dve.wait_ge(S("rstd"), n["sq"])

            def odd_chunk(c, b):
                split()
                slot, uses = ring.back(3)
                dve.wait_ge(S(f"used{slot}"), 2 * uses)
                dve.tensor_scalar(Yo[:, 1, bass.ds(c * 512, 512)], bank(b + 1), rstd[:, k, 1:2], None,
                                  ALU.mult).then_inc(S("pj_dve"), 1)
                split()

            ring.pairs(dve, ODD_IN // 512, odd_chunk)
            n["pj"] += 12
            dve.wait_ge(S("pj_act"), n["pj"])
            dve.wait_ge(S("pj_dve"), n["pj"])
            t1, t2 = ropet[:, 0], ropet[:, 1]
            for m in range(MT):
                cos, sin = over(rope_cos[:, m, 32:160], 1, 4), over(rope_sin[:, m, 32:160], 1, 4)
                for j in range(2):
                    x = cut(Yo[:, m, j * 1024:(j + 1) * 1024], 4, 2, P)
                    x1, x2 = x[:, :, 0, :], x[:, :, 1, :]
                    TT(t1, x2, sin, ALU.mult)
                    step(TT(t2, x1, sin, ALU.mult))
                    TT(x1, x1, cos, ALU.mult)
                    step(TT(x2, x2, cos, ALU.mult))
                    TT(x1, x1, t1, ALU.subtract)
                    TT(x2, x2, t2, ALU.add).then_inc(S("o_rope"), 1)
                    dve.wait_ge(S("o_rope"), 2 * m + j + 1)
            for m in range(MT):
                for b in range(2):
                    dve.wait_ge(S("o_qk_ps"), 4 * m + b + 3)
                    dve.tensor_copy(kTo[:, 4 * b:4 * b + 4, m * P:(m + 1) * P],
                                    cut(bank(4 * (1 - m) + 2 + b), 4, P)).then_inc(S("o_kT"), 1)
            dve.wait_ge(S("table_in"), 16)
            for h in range(4):
                dve.wait_ge(S("o_sc"), h + 1)
                w = table[:, h * 256:(h + 1) * 256]
                TT(att_o[:, h, 0:2, :], cut(ps[:, h, 0:256], 2, P), cut(w, 2, P), ALU.mult)
                TT(att_o[:, h, 2, :], ps[:, h, 256:384], w[:, 0:P], ALU.mult).then_inc(S("o_att"), 1)
            dve.wait_ge(S("gn_in"), 16)
            dve.wait_ge(S("o_silu"), 2)
            for h in range(4):
                dve.wait_ge(S("rstd_h"), 2 + h)
                for m in range(MT):
                    i = 2 * h + m
                    step(dve.scalar_tensor_tensor(o_t[:, m, :], bank((4, 6, 0, 2)[h] + m),
                                                  rstd_h[:, 8 + i:9 + i], gn_o, ALU.mult, ALU.mult))
                    y = Yo[:, m, 4096 + h * 512:4608 + h * 512]
                    TT(y, y, o_t[:, m, :], ALU.mult).then_inc(S("o_y"), 1)
            for part in range(2):
                xt_split()
                for _ in range(3 if part == 0 else 4):
                    split()
            epilogue(acc)

            ffn(3)
            step(TT(ada_t[:], ada_t[:], adab_t[:].unsqueeze(2).to_broadcast([P, 2 * ADA_T, 2]), ALU.add))
            for l in range(2):
                for j in range(2):
                    c = l * ADA_T + (3 * j + 1) * KT
                    g = vec_t[:, (2 * l + j) * KT:(2 * l + j + 1) * KT].unsqueeze(2).to_broadcast([P, KT, 2])
                    dve.scalar_tensor_tensor(mod[:, l, j].rearrange("p v k -> p k v"), ada_t[:, c:c + KT, :], 1.0, g,
                                             ALU.add, ALU.mult)
            gate = ada_t[:, 2 * KT:3 * KT, :]
            step(TT(gate, gate, vec_t[:, 48:56].unsqueeze(2).to_broadcast([P, KT, 2]), ALU.mult))
            ple(1)

            def xn_tile1(h, epilogues, xn):
                dve.wait_ge(S("h_upd"), 4 * epilogues)
                k = n["sq"] % 4
                n["sq"] += 1
                dve.wait_ge(S("rstd"), n["sq"])
                dve.tensor_scalar(xn[:, 1, :], h[:, 1, :], rstd[:, k, 1:2], None, ALU.mult).then_inc(S("xn_dve"), 1)

            def gain_diag(g):
                if n["gain"]:
                    dve.wait_ge(S("gain_ps"), n["gain"])
                else:
                    dve.wait_ge(S("ones_set"), 1)
                n["gain"] += 1
                TT(diag, over(ident, 1, KT), g.unsqueeze(2).to_broadcast([P, KT, P]), ALU.mult).then_inc(S("diag"), 1)

            def last_slab(k):
                slot, uses = ring.back(k)
                return f"used{slot}", 2 * uses

            def gated_add(h, gains, done):
                dve.wait_ge(S("gain_set"), gains)
                dve.wait_ge(S("acc0"), n["epi"] + 1)
                for half in range(2):
                    c = slice(512 * half, 512 * half + 512)
                    for m in range(MT):
                        if half == 0 and m == 1:
                            dve.wait_ge(S(done[0]), done[1])
                        TT(cut(tmp[:], 2, MT, 512)[:, half, m], acc(m)[:, c], gain[:, c],
                           ALU.mult).then_inc(S("acc_free"), 1)
                    dve.wait_ge(S("acc_free"), 4 * n["epi"] + 2 * half + 2)
                    for m in range(MT):
                        TT(h[:, m, c], h[:, m, c], cut(tmp[:], 2, MT, 512)[:, half, m], ALU.add).then_inc(S("h_upd"), 1)
                n["epi"] += 1

            def mlp(l, v, h, ahead=None, last=False):
                base = MLP_STEPS * n["mlp"]
                n["mlp"] += 1
                gain_diag(ada_of(l, 5, v))
                xt_split()
                split()
                if ahead:
                    xn_tile1(*ahead)

                def squared_relu(j):
                    for m in range(MT):
                        dve.wait_ge(S("m_relu"), 2 * j + m + 1)
                        TT(h1[:, m, :], bank(4 + m), relu_s[:, m, :], ALU.mult).then_inc(S("m_h1"), 1)

                def ht_low(j):
                    dve.wait_ge(S("m_ht_hi"), j + 1)
                    TT(ht_lo[:], cut(ps[:, 6:8, :].rearrange("p b n -> p (b n)"), 4, SEQ), ht_hi[:].bitcast(F32),
                       ALU.subtract).then_inc(S("m_ht"), 1)

                def step(i):
                    ht_low(base + i)
                    split()
                    split()
                    squared_relu(base + i + 1)
                    split()
                    split()

                squared_relu(base)
                split()
                ring.loop(dve, MLP_STEPS - 1, 4, step)
                ht_low(base + MLP_STEPS - 1)
                if not last:
                    split()
                    split()
                gated_add(h, n["gain"], last_slab(1 if last else 3))

            xn_tile1(h_lat, 8, xn_lat)
            dve.wait_ge(S("ctx_in"), 16)
            xn_tile1(h_ctx, 8, xn_ctx)
            gain_diag(ada_of(0, 2, 0))
            dve.wait_ge(S("pool_tab_in"), 16)

            def pool_sums(v):
                dve.wait_ge(S("p_t"), 4 * (v + 1))
                w = SEQ + 2 * PAD
                step(TT(B[:, :, 1:w], A[:, :, 0:w - 1], A[:, :, 1:w], ALU.add))
                step(TT(C[:, :, 2:w - 1], B[:, 2:8, 1:w - 2], B[:, 2:8, 3:w], ALU.add))
                step(TT(B[:, 4:8, 4:w - 3], C[:, 2:6, 2:w - 5], C[:, 2:6, 6:w - 1], ALU.add))
                step(TT(C[:, 4:6, 8:w - 8], B[:, 6:8, 4:w - 12], B[:, 6:8, 12:w - 4], ALU.add))
                out_v = pooled[v]
                for g, sums in enumerate((B[:, 0:2], C[:, 0:2], B[:, 4:6], C[:, 4:6])):
                    last = TT(out_v[:, 2 * g:2 * g + 2, :], sums[:, :, PAD:PAD + SEQ], over(inv_cnt[:, g], 1, 2), ALU.mult)
                step(last)
                TT(out_v, out_v, A[:, :, PAD:PAD + SEQ], ALU.subtract).then_inc(S("pooled"), 1)

            pool_sums(0)
            gain_diag(ada_of(0, 2, 1))
            pool_sums(1)
            gated_add(h_lat, 1, ("pool_y", 1))
            xn_tile1(h_lat, 9, xn_lat)
            gated_add(h_ctx, 2, ("pool_y", 2))
            mlp(0, 0, h_lat, ahead=(h_ctx, 10, xn_ctx))
            mlp(0, 1, h_ctx, ahead=(h_lat, 11, xn_lat))

            gain_diag(ada_of(1, 2, 0))
            xt_split()
            split()
            xn_tile1(h_ctx, 12, xn_ctx_att)
            to = [YQK[:, 1, 0:512], YQK[:, 1, 512:1024], YQK[:, 1, 1024:1536], VL[:, 1], YCK[:, 1], VC[:, 1]]

            def head_norm(y, sq, nsq, cols, heads):
                dve.wait_ge(S("a_sq"), nsq)
                dve.tensor_reduce(ssq_h[:, cols], cut_heads(sq), AX_X, ALU.add).then_inc(S("ssq_h"), 1)
                dve.wait_ge(S("rstd_h"), 5 + nsq)
                yh = cut_heads(y)
                step(TT(yh, yh, rstd_h[:, cols].unsqueeze(2).to_broadcast([P, heads, P]), ALU.mult))

            def cut_heads(y):
                return y.rearrange("p m (h d) -> p (m h) d", d=P)

            def norm_lat():
                dve.wait_ge(S("qk_g_in"), 32)
                head_norm(YQK, sq_l, 1, slice(8, 32), 24)
                qs = YQK[:, :, 0:1024].rearrange("p m (h d) -> p m h d", d=P)
                ks = YQK[:, :, 1024:1536].rearrange("p m (h d) -> p m h d", d=P)
                for m in range(MT):
                    TT(qs[:, m], qs[:, m], over(qk_g[:, 0], 1, 8), ALU.mult)
                    last = TT(ks[:, m], ks[:, m], over(qk_g[:, 1], 1, 4), ALU.mult)
                step(last)

            def rope_lat():
                for m in range(MT):
                    x = YQK[:, m].rearrange("p (h s x d) -> p h s x d", h=12, s=2, x=2)
                    x1, x2 = x[:, :, :, 0, :], x[:, :, :, 1, :]
                    tab = cut(const[:, C_AX + m * P:C_AX + (m + 1) * P], 2, 2, 32)
                    cos, sin = over(tab[:, 0], 1, 12), over(tab[:, 1], 1, 12)
                    TT(rope_t[:, 0], x2, sin, ALU.mult)
                    step(TT(rope_t[:, 1], x1, sin, ALU.mult))
                    TT(x1, x1, cos, ALU.mult)
                    step(TT(x2, x2, cos, ALU.mult))
                    TT(x1, x1, rope_t[:, 0], ALU.subtract)
                    last = TT(x2, x2, rope_t[:, 1], ALU.add)
                    if m == 0:
                        step(last)
                last.then_inc(S("a_rope"), 1)

            for c in range(6):
                if c == 4:
                    xt_split()
                    norm_lat()
                if c == 5:
                    head_norm(YCK, sq_c, 2, slice(0, 8), 8)
                    kc8 = cut_heads(YCK)
                    TT(kc8, kc8, over(qk_g[:, 1], 1, 8), ALU.mult).then_inc(S("a_kc"), 1)
                    rope_lat()
                split()
                slot, uses = ring.back(3)
                dve.wait_ge(S(f"used{slot}"), 2 * uses)
                dve.tensor_copy(to[c], bank(5 + 2 * (c % 2))).then_inc(S("pj_dve"), 1)
                split()
            n["pj"] += 6
            for b in range(2, 4):
                dve.wait_ge(S("a_q_ps"), b + 1)
                dve.tensor_copy(qT_a[:, 2 * b:2 * b + 2, :], cut(bank(b), 2, SEQ)).then_inc(S("a_qT"), 1)
            dve.wait_ge(S("a_k_ps"), 2)
            dve.tensor_copy(kT_a[:, 1], cut(ps[:, 6:8, :].rearrange("p b n -> p (b n)"), 4, SEQ)).then_inc(S("a_kT"), 1)

            def maxima(b):
                c = slice(4 * b, 4 * b + 4)
                dve.wait_ge(S("a_sc"), b + 1)
                g0 = 4 * (b % 2)
                step(dve.tensor_reduce(amx[:, c], ps[:, g0:g0 + 4, :], AX_X, ALU.max))
                dve.tensor_scalar(anm[:, c], amx[:, c], -ATT_SCALE, None, ALU.mult).then_inc(S("a_mx"), 1)

            def turned_weights(b):
                for j in (1, 3):
                    dve.wait_ge(S("a_pT"), 4 * b + j + 1)
                    dve.tensor_copy(PT_a[:, b % 2, j], cut(bank(4 * (b % 2) + j), 4, P)).then_inc(S("a_PTd"), 1)

            def normed_out(b):
                c = slice(4 * b, 4 * b + 4)
                dve.wait_ge(S("a_e"), 4 * b + 4)
                step(dve.reciprocal(ard[:, c], asm[:, c]))
                dve.wait_ge(S("a_o"), b + 1)
                TT(cut(OA[:, b // 2, (b % 2) * 512:(b % 2) * 512 + 512], 4, P), cut(bank(4 * (b % 2)), 4, P),
                   ard[:, c].unsqueeze(2).to_broadcast([P, 4, P]), ALU.mult).then_inc(S("a_oa"), 1)

            for b in (0, 2):
                for part in (maxima, turned_weights, normed_out):
                    part(b)
                    part(b + 1)
            xt_split()
            for _ in range(3):
                split()
            gated_add(h_lat, n["gain"], last_slab(3))
            xn_tile1(h_lat, 13, xn_lat)
            mlp(1, 0, h_lat, last=True)
            k = n["sq"] % 4
            n["sq"] += 1
            dve.wait_ge(S("final_g_in"), 16)
            dve.wait_ge(S("rstd"), n["sq"])
            for m in range(MT):
                dve.scalar_tensor_tensor(out_t[:, m], h_lat[:, m], rstd[:, k, m:m + 1], final_g, ALU.mult,
                                         ALU.mult).then_inc(S("out_ready"), 1)

        @block.gpsimd
        def _(pool):
            n = {k: 0 for k in ("sq", "epi", "step")}

            def step(ins):
                n["step"] += 1
                ins.then_inc(S("pool_step"), 1)
                pool.wait_ge(S("pool_step"), n["step"])

            def token_scale(factor=1.0):
                k = n["sq"] % 4
                n["sq"] += 1
                pool.wait_ge(S("ssq"), 2 * n["sq"])
                step(pool.tensor_scalar(rstd[:, k, :], ssq[:, k, :], 1.0 / (D * factor ** 2), EPS / factor ** 2,
                                        ALU.mult, ALU.add))
                pool.tensor_tensor(rstd[:, k, :], rstd[:, k, :], minus_half[:, 0:MT],
                                   ALU.pow).then_inc(S("rstd"), 1)

            def head_scale(cols, width):
                step(pool.tensor_scalar(rstd_h[:, cols], ssq_h[:, cols], 1.0 / width, EPS, ALU.mult, ALU.add))
                pool.tensor_tensor(rstd_h[:, cols], rstd_h[:, cols], minus_half[:, cols],
                                   ALU.pow).then_inc(S("rstd_h"), 1)

            def load_gain(l, j):
                if n["epi"]:
                    pool.wait_ge(S("h_upd"), 4 * n["epi"])
                n["epi"] += 1
                pool.dma_start(gain[:], T["norm_g"][l, j].partition_broadcast(P)).then_inc(S("gain_in"), 16)

            step(pool.memset(minus_half[:], -0.5))
            pool.memset(s4[:].bitcast(F32), 0.0).then_inc(S("s4_zero"), 1)
            load_gain(0, 1)
            for o in range(2):
                pool.dma_start(sink_b[:, 4 * o:4 * o + 4],
                               T["attn_sinks"][0].rearrange("(p o) -> o p", o=2)[o].partition_broadcast(P),
                               allow_slow_non_contiguous=True).then_inc(S("sink_in"), 16)
            pool.dma_start(onorm_b, T["hgrn_onorm_g"][0].partition_broadcast(P)).then_inc(S("onorm_in"), 16)
            pool.dma_start(table[:], T["hgrn_lb"].rearrange("r d -> (r d)").partition_broadcast(P)).then_inc(S("lb_in"), 16)
            token_scale()
            pool.wait_ge(S("const_in"), 16)
            pool.wait_ge(S("pos_in"), 16)
            posf = arena[:, 8192:8194]
            turns = region(8200, MT, 160)
            part = region(8600, MT, 160)
            step(pool.tensor_copy(posf, pos_i[:]))
            ang = rope_sin
            for m in range(MT):
                step(pool.tensor_scalar(ang[:, m, :], const[:, C_INV:C_SEL], posf[:, m:m + 1], None, ALU.mult))
            magic = 12582912.0
            two_pi = (6.28125, 0.0019350051879882812, 3.01991598e-07)
            for quarter, dst in ((0.25, rope_cos), (0.0, rope_sin)):
                step(pool.tensor_scalar(turns, ang[:], 0.15915494309189535, quarter, ALU.mult, ALU.add))
                step(pool.tensor_scalar(turns, turns, magic, None, ALU.add))
                step(pool.tensor_scalar(turns, turns, -magic, None, ALU.add))
                for j, c in enumerate(two_pi):
                    step(pool.tensor_scalar(part, turns, c, None, ALU.mult))
                    step(pool.tensor_tensor(dst[:], ang[:] if j == 0 else dst[:], part, ALU.subtract))
                if quarter:
                    step(pool.tensor_scalar(dst[:], dst[:], 1.5707963267948966, None, ALU.add))
                step(pool.tensor_scalar(dst[:], dst[:], 3.1415925, -3.1415925, ALU.min, ALU.max))
            pool.tensor_copy(posf, posf).then_inc(S("rope_ang"), 1)

            def after_ffn(l, j, factor=0.5):
                token_scale(factor)
                load_gain(l, j)

            after_ffn(0, 3)
            token_scale()
            pool.wait_ge(S("ssq_h"), 1)
            head_scale(slice(0, 8), 128)
            token_scale()
            pool.dma_start(p_in, T["p"][0, 0].rearrange("(m p) d -> p m d", p=P)).then_inc(S("p_in"), 16)
            pool.dma_start(table[:], T["decay_tab"]).then_inc(S("table_in"), 16)
            load_gain(0, 5)
            token_scale()
            after_ffn(0, 6)
            token_scale(0.5)
            load_gain(1, 1)
            token_scale()
            after_ffn(1, 3)
            token_scale()
            pool.wait_ge(S("o_qk_ps"), 8)
            pool.dma_start(gn_o, T["ret_onorm_g"][0].partition_broadcast(P)).then_inc(S("gn_in"), 16)
            for h in range(4):
                pool.wait_ge(S("o_ssq"), 2 * (h + 1))
                head_scale(slice(8 + 2 * h, 10 + 2 * h), 512)
            token_scale()
            pool.dma_start(p_in, T["p"][1, 0].rearrange("(m p) d -> p m d", p=P)).then_inc(S("p_in"), 16)
            load_gain(1, 5)
            token_scale()
            pool.dma_start(pool_w, T["pool_w_2"][0].rearrange("g (k p) n -> p (g k) n", p=P)).then_inc(S("pool_w_in"), 16)
            pool.dma_start(table[:], T["pool_tab"]).then_inc(S("pool_tab_in"), 16)
            pool.memset(ones, 1.0).then_inc(S("ones_set"), 1)
            after_ffn(1, 6)
            token_scale(0.5)
            pool.wait_ge(S("h_upd"), 4 * 8)
            pool.memset(A[:, :, 0:PAD], 0.0)
            pool.memset(A[:, :, PAD + SEQ:], 0.0).then_inc(S("pads"), 1)
            for _ in range(4):
                token_scale()
            pool.wait_ge(S("pooled"), 2)
            pool.dma_start(qk_g[:, 0], T["attn_q_g_2"][0].partition_broadcast(P)).then_inc(S("qk_g_in"), 16)
            pool.dma_start(qk_g[:, 1], T["attn_k_g_2"][0].partition_broadcast(P)).then_inc(S("qk_g_in"), 16)
            for _ in range(2):
                token_scale()
            pool.wait_ge(S("ssq_h"), 2)
            head_scale(slice(8, 32), 128)
            pool.wait_ge(S("ssq_h"), 3)
            head_scale(slice(0, 8), 128)
            pool.wait_ge(S("a_kc"), 1)
            pool.dma_start(final_g, T["final_g_2"].partition_broadcast(P)).then_inc(S("final_g_in"), 16)
            token_scale()
            token_scale()


INPUTS = ("x", "p", "positions", "norm_g", "ffn1_w_in", "ffn1_w_out", "ffn2_w_in", "ffn2_w_out", "ple_w_proj",
          "ple_w_gate", "even_w_in", "even_w_out", "hgrn_lb", "hgrn_onorm_g", "attn_sinks", "odd_w_in", "odd_w_out",
          "ret_onorm_g", "c_2", "ctx_2", "c_ctx_2", "ada_w_2", "ada_b_2", "norm_g_2", "mlp_w1_2", "mlp_w2_2",
          "pool_w_2", "pool_scale_2", "attn_w_qkv_2", "attn_w_o_2", "attn_q_g_2", "attn_k_g_2", "final_g_2")


def kernel(**inputs):
    import concourse.bacc as bacc
    from concourse.bass_utils import run_bass_kernel_spmd

    nc = bacc.Bacc("TRN2", target_bir_lowering=False, num_devices=1)
    const_tab, decay_tab, pool_tab = shape_tables()
    arrays = {name: np.ascontiguousarray(inputs[name]) for name in INPUTS}
    arrays.update(const_tab=const_tab, decay_tab=decay_tab, pool_tab=pool_tab)
    args = {name: nc.dram_tensor(name + "_dram", a.shape, mybir.dt.from_np(a.dtype), kind="ExternalInput").ap()
            for name, a in arrays.items()}
    out = nc.dram_tensor("out_dram", (1, SEQ, D), F32, kind="ExternalOutput").ap()
    build(nc, args, out)
    r = run_bass_kernel_spmd(nc, [{name + "_dram": a for name, a in arrays.items()}], core_ids=[0])
    return r.results[0]["out_dram"]
```
